# Optimizing a Trainium2 kernel written in Bass

```python
import math
import jax, jax.numpy as jnp
from jax import lax
import numpy as np

D_MODEL = 1024
BATCH = 1
SEQ = 256
DEPTH = 1

DIFF_HEADS = D_MODEL // 256
DIFF_QK_DIM = 64
DIFF_V_DIM = 2 * DIFF_QK_DIM
DIFF_WIDTH = DIFF_HEADS * DIFF_V_DIM
MOBA_HEADS = D_MODEL // 128
MOBA_HEAD_DIM = 64
MOBA_WIDTH = MOBA_HEADS * MOBA_HEAD_DIM
MOBA_BLOCK = 256
MOBA_TOPK = 3
MIX_WIDTH = DIFF_WIDTH + MOBA_WIDTH
Q_BLOCK = 128
DIFF_QK_COLS = DIFF_HEADS * 2 * DIFF_QK_DIM
IN_COLS = 2 * DIFF_QK_COLS + DIFF_WIDTH + 3 * MOBA_WIDTH
REL_BUCKETS = 32
REL_MAX_DIST = 128
N_BIAS_COLS = 2 * DIFF_HEADS + MOBA_HEADS
PEER_HEADS = 8
PEER_NKEYS = 128
PEER_N_EXPERTS = PEER_NKEYS * PEER_NKEYS
PEER_KEY_DIM = 128
PEER_TOPK = 16
PEER_CHUNK = 128
NORM_EPS = 1e-6
NEG_INF = -1e30

kernel_name = 'hymba_diffattn_moba_peer_block'

def rmsnorm(x, g):
    xf = x.astype(jnp.float32)
    y = xf * lax.rsqrt(jnp.mean(xf * xf, axis=-1, keepdims=True) + NORM_EPS)
    return (y * g.astype(jnp.float32)).astype(x.dtype)

def t5_bucket(n):
    max_exact = REL_BUCKETS // 2
    nf = jnp.maximum(n, 1).astype(jnp.float32)
    large = max_exact + (jnp.log(nf / max_exact) / math.log(REL_MAX_DIST / max_exact)
                         * (REL_BUCKETS - max_exact)).astype(jnp.int32)
    large = jnp.minimum(large, REL_BUCKETS - 1)
    return jnp.where(n < max_exact, n, large)

def diff_attention(q, k, v, lam, bias_t, lambda_init, subln_g):
    B, S = q.shape[0], q.shape[1]
    H = DIFF_HEADS
    nqb = S // Q_BLOCK
    scale = DIFF_QK_DIM ** -0.5
    qb = q.reshape(B, nqb, Q_BLOCK, H, 2, DIFF_QK_DIM).transpose(1, 0, 3, 4, 2, 5)
    kt = k.transpose(0, 2, 3, 1, 4)
    vt = v.transpose(0, 2, 1, 3)
    kpos = jnp.arange(S)

    def one_block(args):
        qi, i = args
        q_pos = i * Q_BLOCK + jnp.arange(Q_BLOCK)
        dist = q_pos[:, None] - kpos[None, :]
        bias = bias_t[:, :, jnp.clip(dist, 0, S - 1)].astype(jnp.float32)
        logits = jnp.einsum('bhmqd,bhmkd->bhmqk', qi, kt).astype(jnp.float32) * scale + bias[None]
        logits = jnp.where(dist >= 0, logits, NEG_INF)
        p = jax.nn.softmax(logits, axis=-1)
        attn = (p[:, :, 0] - lam * p[:, :, 1]).astype(vt.dtype)
        return jnp.einsum('bhqk,bhkd->bhqd', attn, vt)

    out = lax.map(one_block, (qb, jnp.arange(nqb)))
    out = out.transpose(1, 0, 3, 2, 4).reshape(B, S, H, DIFF_V_DIM)
    out = rmsnorm(out, subln_g) * (1.0 - lambda_init)
    return out.reshape(B, S, H * DIFF_V_DIM)

def moba_attention(q, k, v, bias_t):
    B, S = q.shape[0], q.shape[1]
    H, dh = MOBA_HEADS, MOBA_HEAD_DIM
    nblk = -(-S // MOBA_BLOCK)
    S_pad = nblk * MOBA_BLOCK
    nqb = S // Q_BLOCK
    scale = dh ** -0.5
    qt = q.transpose(0, 2, 1, 3)
    pad = ((0, 0), (0, 0), (0, S_pad - S), (0, 0))
    kb = jnp.pad(k.transpose(0, 2, 1, 3), pad).reshape(B, H, nblk, MOBA_BLOCK, dh)
    vb = jnp.pad(v.transpose(0, 2, 1, 3), pad).reshape(B, H, nblk, MOBA_BLOCK, dh)
    kmean = kb.astype(jnp.float32).mean(axis=3)
    gate = jnp.einsum('bhsd,bhnd->bhsn', qt.astype(jnp.float32), kmean)
    past = jnp.arange(nblk)[None, :] < (jnp.arange(S) // MOBA_BLOCK)[:, None]
    gate = jnp.where(past, gate, NEG_INF)
    ksel = min(MOBA_TOPK, nblk)
    _, sel = lax.top_k(gate, ksel)

    q_items = qt.reshape(B, H, nqb, Q_BLOCK, dh).transpose(0, 2, 1, 3, 4).reshape(B * nqb, H, Q_BLOCK, dh)
    sel_items = sel.reshape(B, H, nqb, Q_BLOCK, ksel).transpose(0, 2, 1, 3, 4).reshape(B * nqb, H, Q_BLOCK, ksel)
    b_ids = jnp.repeat(jnp.arange(B), nqb)
    qb_ids = jnp.tile(jnp.arange(nqb), B)
    head_ids = jnp.arange(H)
    offs = jnp.arange(MOBA_BLOCK)

    def one_item(args):
        qi, si, b, i = args
        kbb, vbb = kb[b], vb[b]
        q_pos = i * Q_BLOCK + jnp.arange(Q_BLOCK)
        own = (i * Q_BLOCK) // MOBA_BLOCK
        k_own = lax.dynamic_index_in_dim(kbb, own, axis=1, keepdims=False)
        v_own = lax.dynamic_index_in_dim(vbb, own, axis=1, keepdims=False)
        k_sel = kbb[head_ids[:, None, None], si]
        v_sel = vbb[head_ids[:, None, None], si]
        dist_sel = q_pos[None, :, None, None] - (si[..., None] * MOBA_BLOCK + offs)
        bias_sel = bias_t[head_ids[:, None, None, None], jnp.clip(dist_sel, 0, S_pad - 1)].astype(jnp.float32)
        l_sel = jnp.einsum('hqd,hqjpd->hqjp', qi, k_sel).astype(jnp.float32) * scale + bias_sel
        l_sel = jnp.where((si < own)[..., None], l_sel, NEG_INF)
        dist_own = q_pos[:, None] - (own * MOBA_BLOCK + offs)[None, :]
        bias_own = bias_t[:, jnp.clip(dist_own, 0, S_pad - 1)].astype(jnp.float32)
        l_own = jnp.einsum('hqd,hpd->hqp', qi, k_own).astype(jnp.float32) * scale + bias_own
        l_own = jnp.where(dist_own >= 0, l_own, NEG_INF)
        logits = jnp.concatenate([l_sel.reshape(H, Q_BLOCK, ksel * MOBA_BLOCK), l_own], axis=-1)
        p = jax.nn.softmax(logits, axis=-1).astype(v.dtype)
        p_sel = p[..., :ksel * MOBA_BLOCK].reshape(H, Q_BLOCK, ksel, MOBA_BLOCK)
        p_own = p[..., ksel * MOBA_BLOCK:]
        return (jnp.einsum('hqjp,hqjpd->hqd', p_sel, v_sel)
                + jnp.einsum('hqp,hpd->hqd', p_own, v_own))

    out = lax.map(one_item, (q_items, sel_items, b_ids, qb_ids))
    out = out.reshape(B, nqb, H, Q_BLOCK, dh).transpose(0, 1, 3, 2, 4)
    return out.reshape(B, S, H * dh)

def peer(h, wq, sub_keys, exp_u, exp_v):
    B, S, D = h.shape
    tokens = h.reshape(-1, PEER_CHUNK, D)

    def chunk(hc):
        T = hc.shape[0]
        q = (hc @ wq).reshape(T, PEER_HEADS, 2, PEER_KEY_DIM)
        s1 = jnp.einsum('thd,hnd->thn', q[:, :, 0], sub_keys[:, 0]).astype(jnp.float32)
        s2 = jnp.einsum('thd,hnd->thn', q[:, :, 1], sub_keys[:, 1]).astype(jnp.float32)
        v1, i1 = lax.top_k(s1, PEER_TOPK)
        v2, i2 = lax.top_k(s2, PEER_TOPK)
        cand = (v1[..., :, None] + v2[..., None, :]).reshape(T, PEER_HEADS, PEER_TOPK * PEER_TOPK)
        sc, ci = lax.top_k(cand, PEER_TOPK)
        e = (jnp.take_along_axis(i1, ci // PEER_TOPK, axis=-1) * PEER_NKEYS
             + jnp.take_along_axis(i2, ci % PEER_TOPK, axis=-1))
        g = jax.nn.softmax(sc, axis=-1)
        u_g = exp_u[e]
        act = jax.nn.gelu(jnp.einsum('td,thkd->thk', hc, u_g).astype(jnp.float32), approximate=False)
        w = (g * act).astype(hc.dtype)
        return jnp.einsum('thk,thkd->td', w, exp_v[e])

    return lax.map(chunk, tokens).reshape(B, S, D)

def setup_inputs(seed: int = 0) -> dict:
    key = jax.random.key(seed)
    ks = jax.random.split(key, 18)
    D = D_MODEL
    f32 = jnp.float32
    nrm = lambda k, shape, s: jax.random.normal(k, shape, f32) * s
    return {
        'x': nrm(ks[0], (BATCH, SEQ, D), 1.0),
        'c': nrm(ks[1], (BATCH, D), 1.0),
        'rel_bias': nrm(ks[2], (REL_BUCKETS, N_BIAS_COLS), 0.5),
        'w_ada': nrm(ks[3], (DEPTH, D, 6 * D), D ** -0.5),
        'b_ada': nrm(ks[4], (DEPTH, 6 * D), 0.02),
        'norm1_g': 1.0 + nrm(ks[5], (DEPTH, D), 0.05),
        'w_in': nrm(ks[6], (DEPTH, D, IN_COLS), D ** -0.5),
        'diff_lambda': nrm(ks[7], (DEPTH, 4, DIFF_QK_DIM), 0.1),
        'diff_subln_g': 1.0 + nrm(ks[8], (DEPTH, DIFF_V_DIM), 0.05),
        'w_out': nrm(ks[9], (DEPTH, MIX_WIDTH, D), MIX_WIDTH ** -0.5),
        'norm2_g': 1.0 + nrm(ks[10], (DEPTH, D), 0.05),
        'peer_wq': nrm(ks[11], (DEPTH, D, PEER_HEADS * 2 * PEER_KEY_DIM), D ** -0.5),
        'peer_keys': nrm(ks[12], (DEPTH, PEER_HEADS, 2, PEER_NKEYS, PEER_KEY_DIM), PEER_KEY_DIM ** -0.5),
        'peer_u': nrm(ks[13], (DEPTH, PEER_N_EXPERTS, D), D ** -0.5),
        'peer_v': nrm(ks[14], (DEPTH, PEER_N_EXPERTS, D), PEER_HEADS ** -0.5),
        'final_g': 1.0 + nrm(ks[15], (D,), 0.05),
    }

def reference(x, c, rel_bias, w_ada, b_ada, norm1_g, w_in, diff_lambda, diff_subln_g,
              w_out, norm2_g, peer_wq, peer_keys, peer_u, peer_v, final_g):
    B, S, D = x.shape
    S_pad = -(-S // MOBA_BLOCK) * MOBA_BLOCK
    bias_by_dist = rel_bias[t5_bucket(jnp.arange(S_pad))]
    diff_bias_t = bias_by_dist[:, :2 * DIFF_HEADS].reshape(S_pad, 2, DIFF_HEADS).transpose(2, 1, 0)
    moba_bias_t = bias_by_dist[:, 2 * DIFF_HEADS:].T
    c_act = jax.nn.silu(c)
    splits = np.cumsum([DIFF_QK_COLS, DIFF_QK_COLS, DIFF_WIDTH, MOBA_WIDTH, MOBA_WIDTH]).tolist()
    for l in range(DEPTH):
        mod = c_act @ w_ada[l] + b_ada[l]
        sh1, sc1, g1, sh2, sc2, g2 = jnp.split(mod, 6, axis=-1)
        h = rmsnorm(x, norm1_g[l]) * (1.0 + sc1[:, None]) + sh1[:, None]
        proj = h @ w_in[l]
        dq, dk, dv, mq, mk, mv = jnp.split(proj, splits, axis=-1)
        lambda_init = 0.8 - 0.6 * math.exp(-0.3 * l)
        lp = diff_lambda[l].astype(jnp.float32)
        lam = jnp.exp(jnp.sum(lp[0] * lp[1])) - jnp.exp(jnp.sum(lp[2] * lp[3])) + lambda_init
        d_out = diff_attention(
            dq.reshape(B, S, DIFF_HEADS, 2, DIFF_QK_DIM),
            dk.reshape(B, S, DIFF_HEADS, 2, DIFF_QK_DIM),
            dv.reshape(B, S, DIFF_HEADS, DIFF_V_DIM),
            lam, diff_bias_t, lambda_init, diff_subln_g[l])
        m_out = moba_attention(
            mq.reshape(B, S, MOBA_HEADS, MOBA_HEAD_DIM),
            mk.reshape(B, S, MOBA_HEADS, MOBA_HEAD_DIM),
            mv.reshape(B, S, MOBA_HEADS, MOBA_HEAD_DIM),
            moba_bias_t)
        mix = jnp.concatenate([d_out, m_out], axis=-1) @ w_out[l]
        x = x + g1[:, None] * mix
        h2 = rmsnorm(x, norm2_g[l]) * (1.0 + sc2[:, None]) + sh2[:, None]
        x = x + g2[:, None] * peer(h2, peer_wq[l], peer_keys[l], peer_u[l], peer_v[l])
    return rmsnorm(x, final_g)


_drawn_inputs = setup_inputs


def setup_inputs(seed=0):
    import zlib

    import numpy as np

    out = dict(_drawn_inputs(seed))
    spreads = {}
    factors = {}
    for name, (base, spread) in spreads.items():
        noise = np.random.default_rng([zlib.crc32(name.encode()), seed]).standard_normal(out[name].shape)
        drawn = base * np.exp(spread * noise) if base else spread * noise
        out[name] = __import__('jax').numpy.asarray(drawn.astype(out[name].dtype))
    for name, factor in factors.items():
        out[name] = (out[name] * factor).astype(out[name].dtype)
    return out
```

```python
from contextlib import ExitStack

import concourse.bass as bass
from concourse import mybir

P = 128
D = 1024
SEQ = 256
DC = D // P
TT = SEQ // P
DIFF_HEADS = 4
MOBA_HEADS = 8
DH = 64
MAPS = 2 * DIFF_HEADS + MOBA_HEADS
PAIRS = MAPS // 2
UNITS = TT * PAIRS
REL_BUCKETS = 32
HEADS = 8
TOPK = 16
HK = HEADS * TOPK
KEYS = 128
LISTS = 2 * HEADS
BLOCKS = 128
HALF = BLOCKS // 2
RAW = 4
PARTS = 4
EXP_AT = 48
GT = 4
GP = 3
EPS = 1e-6
MASKED = -1e30
LAMBDA_INIT = 0.8 - 0.6
QK_SCALE = DH ** -0.5
TABLE = P - 1 + SEQ
LOG_BUCKETS = [16, 19, 21, 24, 27, 31, 35, 40, 46, 52, 59, 67, 77, 87, 99, 113]
PIECE = DC * D

ALU = mybir.AluOpType
ACT = mybir.ActivationFunctionType
AX = mybir.AxisListType
F32 = mybir.dt.float32
F32R = mybir.dt.float32r
BF16 = mybir.dt.bfloat16
U32 = mybir.dt.uint32


def spread(ap, dim, n):
    shape = list(ap.shape)
    shape.insert(dim, n)
    return ap.unsqueeze(dim).broadcast_to(shape)


def hybrid_peer_layer(nc, x, c_col, rel_t, w_ada, cols, b_row, lam, final_g,
                      w_in, w_out, wq, keys_t, u_t, v_b, out):
    base = (nc.sbuf_base + 31) // 32 * 32
    with ExitStack() as ctx:
        ctx.enter_context(nc.sbuf_tensor("arena", [P, 52900], F32))

        def at(name, word, shape, dt=F32):
            return nc.alloc_sbuf_tensor_at(name, shape, dt, offset=base + 4 * word)

        def sem(name):
            return ctx.enter_context(nc.semaphore(name))

        R = [0, PIECE, 2 * PIECE, 3 * PIECE, 4 * PIECE]
        RAW0, X0, M0, G20, S0 = 40960, 45056, 47104, 51200, 52224
        act = at("act", 0, [P, BLOCKS, SEQ])
        sc1_w = at("sc1_w", R[0], [P, DC, D])
        sh1_w = at("sh1_w", R[1], [P, DC, D])
        win = [at("win0", R[2], [P, DC, D]), at("win1", R[4], [P, DC, D]), at("win2", R[0], [P, DC, D])]
        g1_w = at("g1_w", R[1], [P, DC, D])
        sc2_w = at("sc2_w", R[2], [P, DC, D])
        sh2_w = at("sh2_w", R[4], [P, DC, D])
        g2_w = at("g2_w", R[4], [P, DC, D])
        wo = at("wo", R[1], [P, DC, D])
        wqs = [at("wq0", R[2], [P, DC, D]), at("wq1", R[0], [P, DC, D])]
        keys = at("keys", R[1], [P, LISTS, KEYS])
        g1b = at("g1b", R[0], [P, D])
        logit = at("logit", R[0] + 1024, [P, 2, 2, SEQ])
        prob = at("prob", R[0] + 2048, [P, 2, 2, SEQ])
        probT = at("probT", R[0] + 3072, [P, 2, 4, P])
        head_junk = at("head_junk", R[0] + 4096, [P, TT * DIFF_HEADS, P])
        pv = at("pv", R[0] + 5120, [P, TT, D])
        qk = at("qk", R[3], [P, 2 * PAIRS, SEQ])
        nat = at("nat", R[3] + 4096, [P, TT, D])
        acc = at("acc", R[3] + 6144, [P, 2, D])
        score = at("score", R[3], [P, TT, LISTS, KEYS])
        qT = at("qT", R[3] + 4096, [P, LISTS, SEQ])
        cand = at("cand", R[3] + 4096, [P, HEADS, TOPK, TOPK])
        hit = at("hit", R[3] + 6144, [P, HEADS, TOPK, TOPK])
        top_v = at("top_v", R[2], [P, LISTS, TOPK])
        top_iu = at("top_iu", R[2] + 256, [P, LISTS, TOPK], U32)
        top_i = at("top_i", R[2] + 512, [P, LISTS, TOPK])
        best = at("best", R[2] + 768, [P, HEADS, TOPK])
        best_iu = at("best_iu", R[2] + 896, [P, HEADS, TOPK], U32)
        part_u = at("part_u", R[2] + 1024, [P, 2, HEADS, TOPK], U32)
        part = at("part", R[2] + 1280, [P, 2, HEADS, TOPK])
        chosen = at("chosen", R[2] + 1536, [P, TT, 3, HK])
        gsum = at("gsum", R[2] + 2304, [P, TT, HEADS])
        gate = at("gate", R[2] + 2336, [P, TT, HEADS, TOPK])
        final_gb = at("final_gb", 0, [P, D])
        end_junk = at("end_junk", 1024, [P, TT, D])
        peer = at("peer", 4096, [P, TT, D])
        split = at("split", R[4], [P, 2, 2, D], F32R)
        h2r = at("h2r", R[4] + 4096, [P, 2, DC, SEQ], F32R)
        raw = at("raw", RAW0, [P, RAW, D])
        v = at("v", RAW0, [P, TT, D])
        lam_in = at("lam_in", RAW0, [P, 4 * DH])
        lam_t = at("lam_t", RAW0 + 256, [P, 2, DH])
        rel = at("rel", RAW0 + 512, [MAPS, REL_BUCKETS])
        table = at("table", RAW0 + 1024, [MAPS, TABLE])
        hT = at("hT", RAW0 + 2048, [P, DC, SEQ])
        mixT = at("mixT", RAW0 + 2048, [P, DC, SEQ])
        h2T = at("h2T", RAW0 + 2048, [P, DC, SEQ])
        xs = at("xs", X0, [P, TT, D])
        bias = at("bias", M0, [P, MAPS, SEQ])
        brow2 = at("brow2", M0, [1, D])
        wsplit = at("wsplit", M0, [P, 2, 2, SEQ], F32R)
        oh1 = at("oh1", M0 + 1024, [P, 2, GT, KEYS], BF16)
        oh2g = at("oh2g", M0 + 1536, [P, 2, GT, GP, HALF], BF16)
        oh2 = at("oh2", M0 + 2304, [P, 2, GT, HALF], BF16)
        chosenT = at("chosenT", M0 + 2560, [P, 3, SEQ])
        part_b = at("part_b", M0 + 3328, [P, SEQ, GP], BF16)
        keys_b = at("keys_b", M0 + 3712, [P, 2, SEQ], BF16)
        iota_b = at("iota_b", M0 + 3968, [P, P], BF16)
        g2b = at("g2b", G20, [P, D])
        brow1 = at("brow1", G20, [1, D])
        ident = at("ident", S0, [P, P])
        iota = at("iota", S0 + 128, [P, P])
        ones = at("ones", S0 + 256, [P, P])
        small = [S0 + 384]

        def sm(name, shape):
            n = 1
            for s in shape[1:]:
                n *= s
            t = at(name, small[0], shape)
            small[0] += (n + 7) // 8 * 8
            return t

        ccol = sm("ccol", [P, DC])
        cact = sm("cact", [P, DC])
        small_cols = sm("small_cols", [P, 6 * DC + 1])
        bcol = small_cols[:, 0:4 * DC].rearrange("p (n c) -> p n c", n=4)
        gain = small_cols[:, 4 * DC:6 * DC].rearrange("p (n c) -> p n c", n=2)
        sub = small_cols[:, 6 * DC:6 * DC + 1]
        a1 = sm("a1", [P, 2, DC])
        a2 = sm("a2", [P, 2, DC])
        sq = sm("sq", [P, 3, TT])
        rstd = sm("rstd", [P, 3, TT])
        lsum = sm("lsum", [P, 2])
        lexp = sm("lexp", [P, 2])
        neglam = sm("neglam", [P, 1])
        nmax = sm("nmax", [P, UNITS, 2])
        psum_ = sm("psum_", [P, UNITS, 2])
        rsum = sm("rsum", [P, UNITS, 2])
        rlam = sm("rlam", [P, TT * DIFF_HEADS])
        hsq = sm("hsq", [P, TT * DIFF_HEADS])
        hrs = sm("hrs", [P, TT * DIFF_HEADS])
        assert small[0] <= S0 + 676

        banks = ctx.enter_context(nc.psum_tensor("banks", [P, 8, 512], F32))
        bank = [banks[:, n, :] for n in range(8)]
        scratch = nc.dram_tensor("bias_table", [MAPS, TABLE], F32, kind="Internal")

        x_in, c_in, small_in, lam_sem, rel_in, g1row_in, g2row_in, fin_in = map(
            sem, ("x_in", "c_in", "small_in", "lam_sem", "rel_in", "g1row_in", "g2row_in", "fin_in"))
        part_in = [[sem(f"part_in{n}_{e}") for e in range(PARTS)] for n in range(2)]
        names = ("win0", "win1", "win2", "g1", "sc2", "sh2", "wo", "wq0", "g2", "wq1", "keys")
        loaded = {n: sem(f"loaded_{n}") for n in names}
        raw_full = [sem(f"raw_full{n}") for n in range(RAW)]
        table_built, table_out, bias_in, out_done = map(sem, ("table_built", "table_out", "bias_in", "out_done"))
        const_ready, ones_ready, pool_step = map(sem, ("const_ready", "ones_ready", "pool_step"))
        cact_ready, squared, rooted, normed, lam_exp, lam_ready = map(
            sem, ("cact_ready", "squared", "rooted", "normed", "lam_exp", "lam_ready"))
        v_step = sem("v_step")
        rstd_ready, var_ready, acc_ready, mod_ready, mod_read = map(
            sem, ("rstd_ready", "var_ready", "acc_ready", "mod_ready", "mod_read"))
        xT_ready, hT_ready, proj_ready, proj_out = map(sem, ("xT_ready", "hT_ready", "proj_ready", "proj_out"))
        scores_ready, logits_ready, max_ready, exp_done, attn_ready = map(
            sem, ("scores_ready", "logits_ready", "max_ready", "exp_done", "attn_ready"))
        pT_ready, pT_out, pv_done, pv_out, head_sq, nat_ready = map(
            sem, ("pT_ready", "pT_out", "pv_done", "pv_out", "head_sq", "nat_ready"))
        mixT_ready, mixT_out, mix_ready, x1_ready = map(sem, ("mixT_ready", "mixT_out", "mix_ready", "x1_ready"))
        x2T_ready, h2T_ready, h2r_ready = map(sem, ("x2T_ready", "h2T_ready", "h2r_ready"))
        q_ready, q_out, s_ready, s_out = map(sem, ("q_ready", "q_out", "s_ready", "s_out"))
        gate_max, gate_exp, chosen_ready, cT_ready, cT_out = map(
            sem, ("gate_max", "gate_exp", "chosen_ready", "cT_ready", "cT_out"))
        high_ready, low_ready, block_used, act_ready, act_out = map(
            sem, ("high_ready", "low_ready", "block_used", "act_ready", "act_out"))
        oh2_ready, onehot_ready, gates_ready, gates_out = map(sem, ("oh2_ready", "onehot_ready", "gates_ready", "gates_out"))
        wh_ready, wl_ready, peer_ready, x2_ready, final_ready = map(
            sem, ("wh_ready", "wl_ready", "peer_ready", "x2_ready", "final_ready"))

        block = ctx.enter_context(nc.Block())

        PROJ = [(0, 0, ("q", 0)), (0, 256, ("q", 2)), (0, 512, ("k", 0)), (0, 768, ("k", 2)),
                (1, 0, ("v", 0, 0)), (1, 0, ("v", 1, 0)), (1, 512, ("q", 4)), (1, 768, ("q", 6)),
                (2, 0, ("k", 4)), (2, 256, ("k", 6)), (2, 512, ("v", 0, 512)), (2, 512, ("v", 1, 512))]
        ADA = ["sc1", "sh1", "g1", "sc2", "sh2", "g2"]
        ada_w = {"sc1": sc1_w, "sh1": sh1_w, "g1": g1_w, "sc2": sc2_w, "sh2": sh2_w, "g2": g2_w}

        @block.sync
        def _(sp):
            def load(name, dst, src):
                sp.dma_start(dst[:, :, :], src).then_inc(loaded[name], 16)

            sp.dma_start(ccol[:, :], c_col).then_inc(c_in, 16)
            sp.dma_start(xs[:, :, :], x.rearrange("(t p) d -> p t d", p=P)).then_inc(x_in, 16)
            sp.dma_start(small_cols[:, :], cols).then_inc(small_in, 16)
            sp.dma_start(lam_in[:, :], lam.broadcast_to([P, 4 * DH])).then_inc(lam_sem, 16)
            for n, (dst, src) in enumerate(((sc1_w, w_ada[1]), (sh1_w, w_ada[0]))):
                for e in range(PARTS):
                    c = slice(e * DC // PARTS, (e + 1) * DC // PARTS)
                    sp.dma_start(dst[:, c, :], src[:, c, :]).then_inc(part_in[n][e], 16)
            load("win0", win[0], w_in[0])
            load("win1", win[1], w_in[1])
            sp.wait_ge(acc_ready, 1)
            load("win2", win[2], w_in[2])
            sp.wait_ge(acc_ready, 2)
            load("g1", g1_w, w_ada[2])
            sp.wait_ge(proj_ready, 4)
            load("sc2", sc2_w, w_ada[4])
            sp.wait_ge(proj_ready, 8)
            load("sh2", sh2_w, w_ada[3])
            sp.wait_ge(acc_ready, 3)
            load("wo", wo, w_out)
            sp.wait_ge(acc_ready, 4)
            load("wq0", wqs[0], wq[0])
            sp.wait_ge(acc_ready, 5)
            load("g2", g2_w, w_ada[5])
            sp.wait_ge(logits_ready, UNITS)
            sp.dma_start(brow2[:, :], b_row[1:2, :]).then_inc(g2row_in, 16)
            sp.wait_ge(mix_ready, 2 * TT)
            load("keys", keys, keys_t)
            sp.wait_ge(pv_done, UNITS)
            sp.wait_ge(x1_ready, 2 * TT)
            load("wq1", wqs[1], wq[1])
            sp.wait_ge(q_ready, LISTS // 2)
            sp.wait_ge(h2r_ready, 2)
            for n in range(RAW):
                sp.dma_start(raw[:, n, :], u_t[n]).then_inc(raw_full[n], 16)
            with sp.Fori(1, BLOCKS // RAW) as turn:
                i = turn * RAW
                for s in range(RAW):
                    sp.wait_ge(low_ready, i + (s - RAW + 1))
                    sp.dma_start(raw[:, s, :], u_t[bass.ds(i + s, 1)].rearrange("a p d -> (a p) d")
                                 ).then_inc(raw_full[s], 16)
            with sp.Fori(0, BLOCKS // RAW) as turn:
                i = turn * RAW
                for s in range(RAW):
                    sp.wait_ge(low_ready, i + (BLOCKS + s - RAW + 1))
                    sp.dma_start(raw[:, s, :], v_b[bass.ds(i + s, 1)].rearrange("a p d -> (a p) d")
                                 ).then_inc(raw_full[s], 16)
            sp.wait_ge(wl_ready, BLOCKS)
            sp.wait_ge(wh_ready, BLOCKS)
            sp.dma_start(final_gb[:, :], final_g.broadcast_to([P, D])).then_inc(fin_in, 16)
            for t in range(TT):
                sp.wait_ge(final_ready, t + 1)
                sp.dma_start(out[t * P:(t + 1) * P, :], xs[:, t, :]).then_inc(out_done, 16)
            sp.wait_ge(out_done, 16 * TT)

        @block.gpsimd
        def _(pool):
            pool.dma_start(rel[:, :], rel_t).then_inc(rel_in, 16)
            nc.gpsimd.iota(iota[:, :], [[1, P]], base=0, channel_multiplier=0,
                           allow_small_or_imprecise_dtypes=True).then_inc(const_ready, 1)
            nc.gpsimd.memset(ident[:, :], 0.0).then_inc(pool_step, 1)
            pool.wait_ge(pool_step, 1)
            nc.gpsimd.affine_select(out=ident[:, :], in_=ident[:, :], compare_op=ALU.not_equal, fill=1.0,
                                    base=0, pattern=[[-1, P]], channel_multiplier=1).then_inc(const_ready, 1)
            nc.gpsimd.memset(table[:, 0:P - 1], MASKED).then_inc(table_built, 1)
            pool.wait_ge(rel_in, 16)
            half = REL_BUCKETS // 2
            nc.gpsimd.tensor_copy(table[:, P - 1:P - 1 + half], rel[:, 0:half]).then_inc(table_built, 1)
            for n, lo in enumerate(LOG_BUCKETS):
                hi = (LOG_BUCKETS + [SEQ])[n + 1]
                nc.gpsimd.tensor_copy(table[:, P - 1 + lo:P - 1 + hi],
                                      rel[:, half + n:half + n + 1].broadcast_to([MAPS, hi - lo])
                                      ).then_inc(table_built, 1)
            pool.wait_ge(table_built, 2 + len(LOG_BUCKETS))
            pool.dma_start(scratch.ap(), table[:, :]).then_inc(table_out, 16)
            pool.wait_ge(table_out, 16)
            pool.dma_start(bias[:, :, :], bass.AP(tensor=scratch, offset=0, ap=[[1, P], [TABLE, MAPS], [1, SEQ]])
                           ).then_inc(bias_in, 16)

            def low(n, s):
                pool.wait_ge(high_ready, n + 1)
                nc.gpsimd.tensor_tensor(split[:, s % 2, 1, :], raw[:, s, :],
                                        split[:, s % 2, 0, :].bitcast(F32), ALU.subtract).then_inc(low_ready, 1)

            with pool.Fori(0, (2 * BLOCKS) // RAW) as turn:
                i = turn * RAW
                for s in range(RAW):
                    low(i + s, s)

        @block.scalar
        def _(sc):
            sc.dma_start(brow1[:, :], b_row[0:1, :]).then_inc(g1row_in, 16)
            sc.wait_ge(c_in, 16)
            nc.scalar.activation(cact[:, :], ccol[:, :], ACT.Silu).then_inc(cact_ready, 1)

            def norm_x(n, nth):
                for t in range(TT):
                    if n:
                        sc.wait_ge(x1_ready, 2 * (t + 1))
                    nc.scalar.activation(nat[:, t, :], xs[:, t, :], ACT.Square,
                                         accum_out=sq[:, n, t:t + 1]).then_inc(squared, 1)
                sc.wait_ge(var_ready, nth)
                nc.scalar.activation(rstd[:, n, :], sq[:, n, :], ACT.Sqrt).then_inc(rooted, 1)
                sc.wait_ge(rstd_ready, n + 1)
                for t in range(TT):
                    nc.scalar.activation(nat[:, t, :], xs[:, t, :], ACT.Copy,
                                         scale=rstd[:, n, t:t + 1]).then_inc(normed, 1)

            sc.wait_ge(x_in, 16)
            norm_x(0, 1)
            sc.wait_ge(lam_ready, 2)
            nc.scalar.activation(lexp[:, :], lsum[:, :], ACT.Exp).then_inc(lam_exp, 1)
            for g, (piece, col, dst) in enumerate(PROJ):
                sc.wait_ge(proj_ready, g + 1)
                if dst[0] == "v":
                    if g == 4:
                        sc.wait_ge(lam_ready, 2)
                        sc.wait_ge(table_out, 16)
                    nc.scalar.activation(v[:, dst[1], dst[2]:dst[2] + 512], bank[g % 4][:, :],
                                         ACT.Copy).then_inc(proj_out, 1)
                else:
                    at_ = dst[1] if dst[0] == "q" else PAIRS + dst[1]
                    nc.scalar.activation(qk[:, at_:at_ + 2, :].rearrange("p a s -> p (a s)"), bank[g % 4][:, :],
                                         ACT.Copy, scale=QK_SCALE if dst[0] == "q" else 1.0
                                         ).then_inc(proj_out, 1)

            def exps(a):
                nk = (a // PAIRS + 1) * P
                sc.wait_ge(max_ready, a + 1)
                if a >= 2:
                    sc.wait_ge(pT_ready, a - 1)
                for m in range(2):
                    nc.scalar.activation(prob[:, a % 2, m, 0:nk], logit[:, a % 2, m, 0:nk], ACT.Exp,
                                         bias=nmax[:, a, m:m + 1], accum_out=psum_[:, a, m:m + 1]
                                         ).then_inc(exp_done, 1)

            def pT_copy(a):
                t, j = a // PAIRS, a % PAIRS
                n = (t + 1) * (1 if j < DIFF_HEADS else 2)
                sc.wait_ge(pT_ready, a + 1)
                if a >= 2:
                    sc.wait_ge(pv_done, a - 1)
                nc.scalar.activation(probT[:, a % 2, 0:n, :].rearrange("p n q -> p (n q)"),
                                     bank[4 + a % 2][:, 0:n * P], ACT.Copy).then_inc(pT_out, 1)

            def pv_copy(t):
                sc.wait_ge(pv_done, PAIRS * (t + 1))
                nc.scalar.activation(pv[:, t, :], banks[:, 6:8, :].rearrange("p b n -> p (b n)"), ACT.Copy
                                     ).then_inc(pv_out, 1)

            sc.wait_ge(proj_ready, len(PROJ))
            exps(0)
            for a in range(UNITS):
                if a + 1 < UNITS:
                    exps(a + 1)
                pT_copy(a)
                if a % PAIRS == 0 and a:
                    pv_copy(a // PAIRS - 1)
            pv_copy(TT - 1)
            for t in range(TT):
                sc.wait_ge(pv_out, t + 1)
                for h in range(DIFF_HEADS):
                    nc.scalar.activation(head_junk[:, DIFF_HEADS * t + h, :],
                                         pv[:, t, h * P:(h + 1) * P], ACT.Square,
                                         accum_out=hsq[:, DIFF_HEADS * t + h:DIFF_HEADS * t + h + 1]
                                         ).then_inc(head_sq, 1)
            sc.wait_ge(var_ready, 2)
            nc.scalar.activation(hrs[:, :], hsq[:, :], ACT.Sqrt).then_inc(rooted, 1)

            norm_x(1, 3)
            for g in range(LISTS // 2):
                sc.wait_ge(q_ready, g + 1)
                nc.scalar.activation(qT[:, 2 * g:2 * g + 2, :].rearrange("p a s -> p (a s)"), bank[4 + g % 4][:, :],
                                     ACT.Copy).then_inc(q_out, 1)
            for g in range(TT * LISTS // 4):
                t, l = g // 4, 4 * (g % 4)
                sc.wait_ge(s_ready, g + 1)
                nc.scalar.activation(score[:, t, l:l + 4, :].rearrange("p l n -> p (l n)"), bank[g % 4][:, :],
                                     ACT.Copy).then_inc(s_out, 1)

            def high(n, s, i):
                sc.wait_ge(raw_full[s], i * (16 // RAW) + 16)
                if not (isinstance(n, int) and n < 2):
                    sc.wait_ge(block_used, n - 1)
                nc.scalar.activation(split[:, s % 2, 0, :], raw[:, s, :], ACT.Copy).then_inc(high_ready, 1)

            def gelu(n, s):
                sc.wait_ge(block_used, n + 1)
                nc.scalar.activation(act[:, bass.ds(n, 1), :].rearrange("p a s -> p (a s)"),
                                     bank[4 + s % 2][:, 0:SEQ], ACT.Gelu).then_inc(act_out, 1)

            def whigh(j, s):
                nc.scalar.activation(wsplit[:, s % 2, 0, :], act[:, bass.ds(j, 1), :].rearrange("p a s -> p (a s)"),
                                     ACT.Copy).then_inc(wh_ready, 1)

            def u_blocks(i):
                for s in range(RAW):
                    high(i + s, s, i)
                    if not (isinstance(i, int) and i + s == 0):
                        gelu(i + (s - 1), s - 1)

            sc.wait_ge(h2r_ready, 2)
            u_blocks(0)
            with sc.Fori(1, EXP_AT // RAW) as turn:
                i = turn * RAW
                u_blocks(i)
            for t in range(TT):
                sc.wait_ge(gate_max, t + 1)
                nc.scalar.activation(gate[:, t, :, :], gate[:, t, :, :], ACT.Exp).then_inc(gate_exp, 1)
            with sc.Fori(EXP_AT // RAW, HALF // RAW) as turn:
                i = turn * RAW
                u_blocks(i)
            sc.wait_ge(cT_out, TT)
            with sc.Fori(HALF // RAW, BLOCKS // RAW) as turn:
                i = turn * RAW
                u_blocks(i)
            for s in range(RAW):
                high(BLOCKS + s, s, BLOCKS)
                if s == 0:
                    gelu(BLOCKS - 1, RAW - 1)
                    sc.wait_ge(gates_out, HALF)
                whigh(s, s)
            with sc.Fori(1, HALF // RAW) as turn:
                i = turn * RAW
                for s in range(RAW):
                    high(i + (BLOCKS + s), s, i + BLOCKS)
                    whigh(i + s, s)
            sc.wait_ge(gates_out, 2 * HALF)
            with sc.Fori(HALF // RAW, BLOCKS // RAW) as turn:
                i = turn * RAW
                for s in range(RAW):
                    high(i + (BLOCKS + s), s, i + BLOCKS)
                    whigh(i + s, s)
            for t in range(TT):
                sc.wait_ge(x2_ready, 2 * (t + 1))
                nc.scalar.activation(end_junk[:, t, :], xs[:, t, :], ACT.Square,
                                     accum_out=sq[:, 2, t:t + 1]).then_inc(squared, 1)
            sc.wait_ge(var_ready, 4)
            nc.scalar.activation(rstd[:, 2, :], sq[:, 2, :], ACT.Sqrt).then_inc(rooted, 1)

        @block.tensor
        def _(pe):
            def to_columns(src, done):
                for c in range(DC):
                    for t in range(TT):
                        col = (c % 2) * SEQ + t * P
                        last = nc.tensor.transpose(bank[c // 2][:, col:col + P], src[:, t, c * P:(c + 1) * P],
                                                   ident[:, :])
                    last.then_inc(done, 1)

            def mod_column(k, n):
                pe.wait_ge(acc_ready, k + 1)
                for c in range(DC):
                    last = nc.tensor.matmul(bank[7][:, n * DC + c:n * DC + c + 1], acc[:, k % 2, c * P:(c + 1) * P],
                                            ones[:, 0:1], start=True, stop=True)
                last.then_inc(mod_ready, 1)

            def mod_rows(k, brow, b0):
                pe.wait_ge(acc_ready, k + 1)
                for half in range(2):
                    cols = slice(half * 512, half * 512 + 512)
                    nc.tensor.matmul(bank[b0 + half][:, :], ones[:, :], acc[:, k % 2, cols], start=True, stop=False)
                    last = nc.tensor.matmul(bank[b0 + half][:, :], ones[0:1, :], brow[0:1, cols],
                                            start=False, stop=True)
                last.then_inc(mod_ready, 1)

            pe.wait_ge(const_ready, 2)
            pe.wait_ge(normed, TT)
            to_columns(nat, xT_ready)
            pe.wait_ge(ones_ready, 1)
            mod_column(0, 0)
            mod_column(1, 1)
            pe.wait_ge(hT_ready, DC)
            for g, (piece, col, dst) in enumerate(PROJ):
                pe.wait_ge(loaded[f"win{piece}"], 16)
                if g >= 4:
                    pe.wait_ge(proj_out, g - 3)
                if dst[0] == "v":
                    for c in range(DC):
                        last = nc.tensor.matmul(bank[g % 4][:, :], hT[:, c, dst[1] * P:dst[1] * P + P],
                                                win[piece][:, c, col:col + 512], start=(c == 0), stop=(c == DC - 1))
                else:
                    for e in range(2):
                        for c in range(DC):
                            last = nc.tensor.matmul(bank[g % 4][:, e * SEQ:(e + 1) * SEQ],
                                                    win[piece][:, c, col + e * P:col + e * P + P], hT[:, c, :],
                                                    start=(c == 0), stop=(c == DC - 1))
                last.then_inc(proj_ready, 1)
                if g == 8:
                    pe.wait_ge(g1row_in, 16)
                    mod_rows(2, brow1, 4)
                if g == 10:
                    mod_column(3, 2)
            mod_column(4, 3)

            def scores(a):
                t, j = a // PAIRS, a % PAIRS
                nk = (t + 1) * P
                if a >= 2:
                    pe.wait_ge(logits_ready, a - 1)
                for m in range(2):
                    rows = slice(m * DH, (m + 1) * DH)
                    last = nc.tensor.matmul(bank[a % 2 * 2 + m][:, 0:nk], qk[rows, j, t * P:(t + 1) * P],
                                            qk[rows, PAIRS + j, 0:nk], start=True, stop=True)
                last.then_inc(scores_ready, 1)

            def transposes(a):
                t, j = a // PAIRS, a % PAIRS
                pe.wait_ge(attn_ready, a + 1)
                if a >= 2:
                    pe.wait_ge(pT_out, a - 1)
                for m in range(1 if j < DIFF_HEADS else 2):
                    for kb in range(t + 1):
                        n = m * (t + 1) + kb
                        last = nc.tensor.transpose(bank[4 + a % 2][:, n * P:(n + 1) * P],
                                                   prob[:, a % 2, m, kb * P:(kb + 1) * P], ident[:, :])
                last.then_inc(pT_ready, 1)

            def weigh(a):
                t, j = a // PAIRS, a % PAIRS
                pe.wait_ge(pT_out, a + 1)
                if a == PAIRS:
                    pe.wait_ge(pv_out, 1)
                for m in range(1 if j < DIFF_HEADS else 2):
                    w, c0 = (P, j * P) if j < DIFF_HEADS else (DH, (2 * (j - DIFF_HEADS) + m) * DH)
                    v0 = c0 if j < DIFF_HEADS else 512 + c0
                    for kb in range(t + 1):
                        last = nc.tensor.matmul(bank[6 + (j >= DIFF_HEADS)][:, c0:c0 + w],
                                                probT[:, a % 2, m * (t + 1) + kb, :], v[:, kb, v0:v0 + w],
                                                start=(kb == 0), stop=(kb == t))
                last.then_inc(pv_done, 1)

            pe.wait_ge(proj_out, len(PROJ))
            scores(0)
            scores(1)
            pe.wait_ge(mod_read, 3)
            for a in range(UNITS):
                transposes(a)
                if a + 2 < UNITS:
                    scores(a + 2)
                if a >= 1:
                    weigh(a - 1)
            weigh(UNITS - 1)

            pe.wait_ge(nat_ready, 2 * TT)
            to_columns(nat, mixT_ready)
            pe.wait_ge(loaded["wo"], 16)
            pe.wait_ge(mixT_out, DC)
            for g in range(2 * TT):
                t, half = g // 2, g % 2
                for c in range(DC):
                    last = nc.tensor.matmul(bank[4 + g][:, :], mixT[:, c, t * P:(t + 1) * P],
                                            wo[:, c, half * 512:half * 512 + 512], start=(c == 0), stop=(c == DC - 1))
                last.then_inc(mix_ready, 1)
            pe.wait_ge(g2row_in, 16)
            mod_rows(5, brow2, 0)
            pe.wait_ge(normed, 2 * TT)
            pe.wait_ge(mod_read, 4)
            to_columns(nat, x2T_ready)

            pe.wait_ge(h2T_ready, DC)
            for g in range(LISTS // 2):
                pe.wait_ge(loaded[f"wq{2 * g // DC}"], 16)
                if g >= 4:
                    pe.wait_ge(q_out, g - 3)
                for e in range(2):
                    col = (2 * g + e) % DC * P
                    for c in range(DC):
                        last = nc.tensor.matmul(bank[4 + g % 4][:, e * SEQ:(e + 1) * SEQ],
                                                wqs[2 * g // DC][:, c, col:col + P], h2T[:, c, :],
                                                start=(c == 0), stop=(c == DC - 1))
                last.then_inc(q_ready, 1)
            pe.wait_ge(loaded["keys"], 16)
            pe.wait_ge(q_out, LISTS // 2)
            for g in range(TT * LISTS // 4):
                t = g // 4
                if g >= 4:
                    pe.wait_ge(s_out, g - 3)
                for e in range(4):
                    l = 4 * (g % 4) + e
                    last = nc.tensor.matmul(bank[g % 4][:, e * P:(e + 1) * P], qT[:, l, t * P:(t + 1) * P],
                                            keys[:, l, :], start=True, stop=True)
                last.then_inc(s_ready, 1)

            def u_block(n, s):
                pe.wait_ge(high_ready, n + 1)
                if not (isinstance(n, int) and n < 2):
                    pe.wait_ge(act_out, n - 1)
                dst = bank[4 + s % 2][:, 0:SEQ]
                for c in range(DC):
                    w = split[:, s % 2, 0, c * P:(c + 1) * P]
                    nc.tensor.matmul(dst, w, h2r[:, 0, c, :], start=(c == 0), stop=False)
                    nc.tensor.matmul(dst, w, h2r[:, 1, c, :], start=False, stop=False)
                pe.wait_ge(low_ready, n + 1)
                for c in range(DC):
                    last = nc.tensor.matmul(dst, split[:, s % 2, 1, c * P:(c + 1) * P], h2r[:, 0, c, :],
                                            start=False, stop=(c == DC - 1))
                last.then_inc(block_used, 1)

            def gates(n, s):
                pe.wait_ge(onehot_ready, n + 1)
                if not (isinstance(n, int) and n < 2):
                    pe.wait_ge(gates_out, n - 1)
                for k in range(GT):
                    for e in range(GP):
                        last = nc.tensor.matmul(bank[6 + s % 2][:, k * HALF:(k + 1) * HALF], oh1[:, s % 2, k, :],
                                                oh2g[:, s % 2, k, e, :], start=(e == 0), stop=(e == GP - 1))
                last.then_inc(gates_ready, 1)

            def v_block(j, s, first=False, last_block=False):
                pe.wait_ge(high_ready, j + (BLOCKS + 1))
                pe.wait_ge(wh_ready, j + 1)
                pe.wait_ge(wl_ready, j + 1)
                for t in range(TT):
                    for e in range(2):
                        for half in range(2):
                            nc.tensor.matmul(bank[2 * t + half][:, :], wsplit[:, s % 2, e, t * P:(t + 1) * P],
                                             split[:, s % 2, 0, half * 512:half * 512 + 512],
                                             start=first and e == 0, stop=False, skip_group_check=True)
                pe.wait_ge(low_ready, j + (BLOCKS + 1))
                for t in range(TT):
                    for half in range(2):
                        last = nc.tensor.matmul(bank[2 * t + half][:, :], wsplit[:, s % 2, 0, t * P:(t + 1) * P],
                                                split[:, s % 2, 1, half * 512:half * 512 + 512],
                                                start=False, stop=last_block, skip_group_check=True)
                last.then_inc(block_used, 1)

            pe.wait_ge(h2r_ready, 2)
            for s in range(RAW):
                u_block(s, s)
            with pe.Fori(1, HALF // RAW) as turn:
                i = turn * RAW
                for s in range(RAW):
                    u_block(i + s, s)
            for t in range(TT):
                pe.wait_ge(chosen_ready, 1)
                for k in range(3):
                    last = nc.tensor.transpose(bank[6 + t][:, k * P:(k + 1) * P], chosen[:, t, k, :], ident[:, :])
                last.then_inc(cT_ready, 1)
            pe.wait_ge(cT_out, TT)
            for s in range(RAW):
                u_block(HALF + s, s)
                gates(s, s)
            with pe.Fori(1, HALF // RAW) as turn:
                i = turn * RAW
                for s in range(RAW):
                    u_block(i + (HALF + s), s)
                    gates(i + s, s)
            pe.wait_ge(s_out, TT * LISTS // 4)
            for s in range(RAW):
                v_block(s, s, first=(s == 0))
                gates(HALF + s, s)
            with pe.Fori(1, HALF // RAW) as turn:
                i = turn * RAW
                for s in range(RAW):
                    v_block(i + s, s)
                    gates(i + (HALF + s), s)
            with pe.Fori(HALF // RAW, (BLOCKS - RAW) // RAW) as turn:
                i = turn * RAW
                for s in range(RAW):
                    v_block(i + s, s)
            for s in range(RAW):
                v_block(BLOCKS - RAW + s, s, last_block=(s == RAW - 1))
            pe.wait_ge(block_used, 2 * BLOCKS)
            pe.nop().then_inc(peer_ready, 1)

        @block.vector
        def _(ve):
            steps = [0]

            def link(ins):
                steps[0] += 1
                ins.then_inc(v_step, 1)
                ve.wait_ge(v_step, steps[0])

            def ada(k):
                w = ada_w[ADA[k]]
                ve.wait_ge(loaded[ADA[k]] if k >= 2 else part_in[k][0], 16)
                if k >= 2:
                    ve.wait_ge(mod_ready, k - 1)
                nc.vector.tensor_scalar(acc[:, k % 2, :], w[:, 0, :], cact[:, 0:1], None, ALU.mult
                                        ).then_inc(v_step, 1)
                steps[0] += 1
                for c in range(1, DC):
                    if k < 2 and c % (DC // PARTS) == 0:
                        ve.wait_ge(part_in[k][c * PARTS // DC], 16)
                    ve.wait_ge(v_step, steps[0])
                    ins = nc.vector.scalar_tensor_tensor(out=acc[:, k % 2, :], in0=w[:, c, :],
                                                         scalar=cact[:, c:c + 1], in1=acc[:, k % 2, :],
                                                         op0=ALU.mult, op1=ALU.add)
                    if c < DC - 1:
                        ins.then_inc(v_step, 1)
                        steps[0] += 1
                ins.then_inc(acc_ready, 1)

            def root(n, nth, count):
                ve.wait_ge(squared, count)
                nc.vector.tensor_scalar(sq[:, n, :], sq[:, n, :], 1.0 / D, EPS, ALU.mult, ALU.add
                                        ).then_inc(var_ready, 1)
                ve.wait_ge(rooted, nth)
                nc.vector.reciprocal(rstd[:, n, :], rstd[:, n, :]).then_inc(rstd_ready, 1)

            def modulate(a, n):
                cols = bank[7][:, 2 * n * DC:2 * (n + 1) * DC].rearrange("p (a c) -> p a c", a=2)
                link(nc.vector.tensor_tensor(a[:, :, :], cols, bcol[:, 2 * n:2 * n + 2, :], ALU.add))
                link(nc.vector.scalar_tensor_tensor(out=a[:, 0, :], in0=a[:, 0, :], scalar=1.0, in1=gain[:, n, :],
                                                    op0=ALU.add, op1=ALU.mult))

            def normed_columns(dst, a, src_ready, dst_ready):
                for c in range(DC):
                    ve.wait_ge(src_ready, c // 2 * 2 + 2)
                    nc.vector.tensor_scalar(dst[:, c, :], bank[c // 2][:, (c % 2) * SEQ:(c % 2 + 1) * SEQ],
                                            a[:, 0, c:c + 1], a[:, 1, c:c + 1], ALU.mult, ALU.add
                                            ).then_inc(dst_ready, 1)

            nc.vector.memset(ones[:, :], 1.0).then_inc(ones_ready, 1)
            ve.wait_ge(lam_sem, 16)
            for n in range(2):
                nc.vector.tensor_tensor_reduce(out=lam_t[:, n, :], in0=lam_in[:, 2 * n * DH:(2 * n + 1) * DH],
                                               in1=lam_in[:, (2 * n + 1) * DH:(2 * n + 2) * DH], scale=1.0,
                                               scalar=0.0, op0=ALU.mult, op1=ALU.add,
                                               accum_out=lsum[:, n:n + 1]).then_inc(lam_ready, 1)
            root(0, 1, TT)
            ve.wait_ge(cact_ready, 1)
            ada(0)
            ada(1)
            ve.wait_ge(lam_exp, 1)
            link(nc.vector.scalar_tensor_tensor(out=neglam[:, :], in0=lexp[:, 1:2], scalar=-LAMBDA_INIT,
                                                in1=lexp[:, 0:1], op0=ALU.add, op1=ALU.subtract))
            ve.wait_ge(small_in, 16)
            ve.wait_ge(mod_ready, 2)
            modulate(a1, 0)
            normed_columns(hT, a1, xT_ready, hT_ready)
            ada(2)
            ada(3)
            ada(4)
            ve.wait_ge(proj_ready, len(PROJ))
            for half in range(2):
                link(nc.vector.tensor_copy(g1b[:, half * 512:half * 512 + 512], bank[4 + half][:, :]))
            ve.wait_ge(mod_ready, 5)
            modulate(a2, 1)
            ve.sem_inc(mod_read, 3)

            def logits(a):
                t, j = a // PAIRS, a % PAIRS
                nk = (t + 1) * P
                ve.wait_ge(scores_ready, a + 1)
                if a >= 2:
                    ve.wait_ge(exp_done, 2 * (a - 1))
                nc.vector.tensor_tensor(logit[:, a % 2, :, 0:nk],
                                        banks[:, a % 2 * 2:a % 2 * 2 + 2, 0:nk],
                                        bias[:, 2 * j:2 * j + 2, 0:nk][:, :, ::-1],
                                        ALU.add).then_inc(logits_ready, 1)
                ve.wait_ge(logits_ready, a + 1)
                nc.vector.tensor_reduce(nmax[:, a, :], logit[:, a % 2, :, 0:nk], AX.X, ALU.max,
                                        negate=True).then_inc(max_ready, 1)

            def combine(a):
                t, j = a // PAIRS, a % PAIRS
                nk = (t + 1) * P
                ve.wait_ge(exp_done, 2 * (a + 1))
                inv = nc.vector.reciprocal(rsum[:, a, :], psum_[:, a, :])
                if j >= DIFF_HEADS:
                    inv.then_inc(attn_ready, 1)
                    return
                link(inv)
                h = t * DIFF_HEADS + j
                link(nc.vector.tensor_scalar(rlam[:, h:h + 1], rsum[:, a, 1:2], neglam[:, 0:1], None, ALU.mult))
                link(nc.vector.tensor_scalar(prob[:, a % 2, 1, 0:nk], prob[:, a % 2, 1, 0:nk], rlam[:, h:h + 1],
                                             None, ALU.mult))
                nc.vector.scalar_tensor_tensor(out=prob[:, a % 2, 0, 0:nk], in0=prob[:, a % 2, 0, 0:nk],
                                               scalar=rsum[:, a, 0:1], in1=prob[:, a % 2, 1, 0:nk],
                                               op0=ALU.mult, op1=ALU.add).then_inc(attn_ready, 1)

            ve.wait_ge(bias_in, 16)
            logits(0)
            for a in range(UNITS):
                if a + 1 < UNITS:
                    logits(a + 1)
                combine(a)

            ve.wait_ge(attn_ready, UNITS)
            for t in range(TT):
                ve.wait_ge(pv_out, t + 1)
                inv = rsum[:, PAIRS * t + DIFF_HEADS:PAIRS * (t + 1), :].rearrange("p j m -> p (j m)")
                nc.vector.tensor_tensor(nat[:, t, 512:D].rearrange("p (h d) -> p h d", d=DH),
                                        pv[:, t, 512:D].rearrange("p (h d) -> p h d", d=DH),
                                        spread(inv, 2, DH), ALU.mult).then_inc(nat_ready, 1)
            ve.wait_ge(head_sq, TT * DIFF_HEADS)
            nc.vector.tensor_scalar(hsq[:, :], hsq[:, :], 1.0 / P, EPS, ALU.mult, ALU.add).then_inc(var_ready, 1)
            ve.wait_ge(rooted, 2)
            link(nc.vector.reciprocal(hrs[:, :], hrs[:, :]))
            for t in range(TT):
                nc.vector.tensor_tensor(nat[:, t, 0:512].rearrange("p (h d) -> p h d", d=P),
                                        pv[:, t, 0:512].rearrange("p (h d) -> p h d", d=P),
                                        spread(hrs[:, t * DIFF_HEADS:(t + 1) * DIFF_HEADS], 2, P), ALU.mult
                                        ).then_inc(nat_ready, 1)
            for c in range(DC):
                src = bank[c // 2][:, (c % 2) * SEQ:(c % 2 + 1) * SEQ]
                ve.wait_ge(mixT_ready, c // 2 * 2 + 2)
                if c < DIFF_HEADS:
                    nc.vector.tensor_scalar(mixT[:, c, :], src, sub[:, 0:1], 1.0 - LAMBDA_INIT, ALU.mult, ALU.mult
                                            ).then_inc(mixT_out, 1)
                else:
                    nc.vector.tensor_copy(mixT[:, c, :], src).then_inc(mixT_out, 1)
            ada(5)
            for g in range(2 * TT):
                t, cols = g // 2, slice(g % 2 * 512, g % 2 * 512 + 512)
                ve.wait_ge(mix_ready, g + 1)
                link(nc.vector.tensor_tensor(nat[:, t, cols], bank[4 + g][:, :], g1b[:, cols], ALU.mult))
                nc.vector.tensor_tensor(xs[:, t, cols], xs[:, t, cols], nat[:, t, cols], ALU.add
                                        ).then_inc(x1_ready, 1)
            ve.wait_ge(mod_ready, 6)
            for half in range(2):
                link(nc.vector.tensor_copy(g2b[:, half * 512:half * 512 + 512], bank[half][:, :]))
            ve.sem_inc(mod_read, 1)
            root(1, 3, 2 * TT)
            normed_columns(h2T, a2, x2T_ready, h2T_ready)
            ve.wait_ge(h2T_ready, DC)
            ve.wait_ge(acc_ready, 6)
            nc.vector.tensor_copy(h2r[:, 0, :, :], h2T[:, :, :]).then_inc(h2r_ready, 1)
            ve.wait_ge(h2r_ready, 1)
            nc.vector.tensor_tensor(h2r[:, 1, :, :], h2T[:, :, :], h2r[:, 0, :, :].bitcast(F32), ALU.subtract
                                    ).then_inc(h2r_ready, 1)

            def top16(vals, idx, src, n):
                for k in range(0, TOPK, 8):
                    for l in range(n):
                        last = nc.vector.max(vals[:, l, k:k + 8], src(l))
                    link(last)
                    for l in range(n):
                        last = nc.vector.max_index(idx[:, l, k:k + 8], vals[:, l, k:k + 8], src(l))
                    link(last)
                    if k + 8 < TOPK:
                        for l in range(n):
                            last = nc.vector.match_replace(src(l), vals[:, l, k:k + 8], src(l), -3.0e38)
                        link(last)

            for t in range(TT):
                ve.wait_ge(s_out, (t + 1) * LISTS // 4)
                if t == 0:
                    ve.wait_ge(s_ready, TT * LISTS // 4)
                top16(top_v, top_iu, lambda l: score[:, t, l, :], LISTS)
                link(nc.vector.tensor_copy(top_i[:, :, :], top_iu[:, :, :]))
                halves_v = top_v[:, :, :].rearrange("p (h two) k -> p two h k", two=2)
                halves_i = top_i[:, :, :].rearrange("p (h two) k -> p two h k", two=2)
                link(nc.vector.tensor_tensor(cand[:, :, :, :], spread(halves_v[:, 0], 3, TOPK),
                                             spread(halves_v[:, 1], 2, TOPK), ALU.add))
                top16(best, best_iu, lambda h: cand[:, h, :, :].rearrange("p a b -> p (a b)"), HEADS)
                nc.vector.tensor_tensor(gate[:, t, :, :], best[:, :, :],
                                        best[:, :, 0:1].broadcast_to([P, HEADS, TOPK]), ALU.subtract
                                        ).then_inc(gate_max, 1)
                nc.vector.tensor_scalar(part_u[:, 0, :, :], best_iu[:, :, :], 4, None, ALU.logical_shift_right)
                link(nc.vector.tensor_scalar(part_u[:, 1, :, :], best_iu[:, :, :], TOPK - 1, None,
                                             ALU.bitwise_and))
                link(nc.vector.tensor_copy(part[:, :, :, :], part_u[:, :, :, :]))
                for half in range(2):
                    place = spread(spread(iota[:, 0:TOPK], 1, TOPK), 1, HEADS)
                    link(nc.vector.tensor_tensor(hit[:, :, :, :], spread(part[:, half], 3, TOPK), place,
                                                 ALU.is_equal))
                    link(nc.vector.tensor_tensor(hit[:, :, :, :], hit[:, :, :, :],
                                                 spread(halves_i[:, half], 2, TOPK), ALU.mult))
                    link(nc.vector.tensor_reduce(chosen[:, t, half, :], hit[:, :, :, :], AX.X, ALU.add))
            ve.wait_ge(gate_exp, TT)
            link(nc.vector.tensor_reduce(gsum[:, :, :], gate[:, :, :, :], AX.X, ALU.add))
            link(nc.vector.reciprocal(gsum[:, :, :], gsum[:, :, :]))
            nc.vector.tensor_tensor(chosen[:, :, 2, :].rearrange("p t (h k) -> p t h k", k=TOPK),
                                    gate[:, :, :, :], spread(gsum[:, :, :], 3, TOPK), ALU.mult
                                    ).then_inc(chosen_ready, 1)
            for t in range(TT):
                ve.wait_ge(cT_ready, t + 1)
                nc.vector.tensor_copy(chosenT[:, :, t * P:(t + 1) * P],
                                      bank[6 + t][:, 0:3 * P].rearrange("p (k q) -> p k q", k=3)
                                      ).then_inc(cT_out, 1)
            ve.wait_ge(cT_out, TT)
            nc.vector.tensor_copy(iota_b[:, :], iota[:, :])
            link(nc.vector.tensor_copy(keys_b[:, :, :], chosenT[:, 0:2, :]))
            for e in range(GP):
                link(nc.vector.tensor_copy(part_b[:, :, e], chosenT[:, 2, :]))
                if e < GP - 1:
                    link(nc.vector.tensor_tensor(chosenT[:, 2, :], chosenT[:, 2, :], part_b[:, :, e],
                                                 ALU.subtract))

            def onehots(q, s, half):
                n = q + half * HALF
                if not (isinstance(n, int) and n < 2):
                    ve.wait_ge(gates_ready, n - 1)
                toks = bass.ds(q * GT, GT)
                nc.vector.tensor_tensor(oh2[:, s % 2, :, :], spread(iota_b[:, half * HALF:(half + 1) * HALF], 1, GT),
                                        spread(keys_b[:, 1, toks], 2, HALF), ALU.is_equal).then_inc(oh2_ready, 1)
                nc.vector.tensor_tensor(oh1[:, s % 2, :, :], spread(iota_b[:, :], 1, GT),
                                        spread(keys_b[:, 0, toks], 2, KEYS), ALU.is_equal)
                ve.wait_ge(oh2_ready, n + 1)
                nc.vector.tensor_tensor(oh2g[:, s % 2, :, :, :], spread(oh2[:, s % 2, :, :], 2, GP),
                                        spread(part_b[:, toks, :], 3, HALF), ALU.mult).then_inc(onehot_ready, 1)

            def gate_acts(q, s, half):
                ve.wait_ge(gates_ready, q + (half * HALF + 1))
                dst = act[:, half * HALF:(half + 1) * HALF, bass.ds(q * GT, GT)]
                nc.vector.tensor_tensor(dst, bank[6 + s % 2][:, 0:GT * HALF].rearrange("p (k j) -> p j k", k=GT),
                                        dst, ALU.mult).then_inc(gates_out, 1)

            def wlow(j, s):
                ve.wait_ge(wh_ready, j + 1)
                nc.vector.tensor_tensor(wsplit[:, s % 2, 1, :], act[:, bass.ds(j, 1), :].rearrange("p a s -> p (a s)"),
                                        wsplit[:, s % 2, 0, :].bitcast(F32), ALU.subtract).then_inc(wl_ready, 1)

            ve.wait_ge(act_out, HALF)
            for s in range(RAW):
                onehots(s, s, 0)
                if s:
                    gate_acts(s - 1, s - 1, 0)
            with ve.Fori(1, HALF // RAW) as turn:
                q = turn * RAW
                for s in range(RAW):
                    onehots(q + s, s, 0)
                    gate_acts(q + (s - 1), s - 1, 0)
            gate_acts(HALF - 1, RAW - 1, 0)
            ve.wait_ge(gates_out, HALF)
            ve.wait_ge(act_out, BLOCKS)
            for s in range(RAW):
                wlow(s, s)
                onehots(s, s, 1)
                if s:
                    gate_acts(s - 1, s - 1, 1)
            with ve.Fori(1, HALF // RAW) as turn:
                q = turn * RAW
                for s in range(RAW):
                    wlow(q + s, s)
                    onehots(q + s, s, 1)
                    gate_acts(q + (s - 1), s - 1, 1)
            gate_acts(HALF - 1, RAW - 1, 1)
            ve.wait_ge(gates_out, 2 * HALF)
            with ve.Fori(HALF // RAW, BLOCKS // RAW) as turn:
                j = turn * RAW
                for s in range(RAW):
                    wlow(j + s, s)

            ve.wait_ge(peer_ready, 1)
            ve.wait_ge(wl_ready, BLOCKS)
            for g in range(2 * TT):
                t, cols = g // 2, slice(g % 2 * 512, g % 2 * 512 + 512)
                link(nc.vector.tensor_tensor(peer[:, t, cols], bank[g][:, :], g2b[:, cols], ALU.mult))
                nc.vector.tensor_tensor(xs[:, t, cols], xs[:, t, cols], peer[:, t, cols], ALU.add
                                        ).then_inc(x2_ready, 1)
            root(2, 4, 3 * TT)
            ve.wait_ge(fin_in, 16)
            ve.wait_ge(rstd_ready, 3)
            for t in range(TT):
                nc.vector.scalar_tensor_tensor(out=xs[:, t, :], in0=xs[:, t, :], scalar=rstd[:, 2, t:t + 1],
                                               in1=final_gb[:, :], op0=ALU.mult, op1=ALU.mult
                                               ).then_inc(final_ready, 1)


def kernel(x, c, rel_bias, w_ada, b_ada, norm1_g, w_in, diff_lambda, diff_subln_g,
           w_out, norm2_g, peer_wq, peer_keys, peer_u, peer_v, final_g):
    import numpy as np
    import concourse.bacc as bacc
    from concourse.bass_utils import run_bass_kernel_spmd

    def wide(w):
        w = np.asarray(w)
        return np.ascontiguousarray(w.reshape(DC, P, -1, D).transpose(2, 1, 0, 3))

    def column(w):
        w = np.asarray(w)
        return np.ascontiguousarray(np.moveaxis(w.reshape(w.shape[:-1] + (DC, P)), -1, 0))

    maps = [m * DIFF_HEADS + j for j in range(DIFF_HEADS) for m in range(2)] + list(range(8, MAPS))
    b = np.asarray(b_ada)[0].reshape(6, D)
    rows = {
        "x": np.asarray(x)[0],
        "c_col": column(np.asarray(c)[0]),
        "rel_t": np.ascontiguousarray(np.asarray(rel_bias)[:, maps].T),
        "w_ada": wide(w_ada[0]),
        "b_row": np.ascontiguousarray(b[[2, 5]]),
        "cols": np.concatenate([column(b[[1, 0, 4, 3]]).reshape(P, -1), column(np.asarray(norm1_g)[0]),
                                column(np.asarray(norm2_g)[0]), np.asarray(diff_subln_g)[0].reshape(P, 1)], 1),
        "lam": np.ascontiguousarray(np.asarray(diff_lambda).reshape(1, 4 * DH)),
        "final_g": np.ascontiguousarray(np.asarray(final_g).reshape(1, D)),
        "w_in": wide(w_in[0]),
        "w_out": wide(w_out[0])[0],
        "wq": wide(peer_wq[0]),
        "keys_t": np.ascontiguousarray(np.asarray(peer_keys)[0].reshape(LISTS, KEYS, P).transpose(2, 0, 1)),
        "u_t": np.ascontiguousarray(np.asarray(peer_u)[0].reshape(P, BLOCKS, DC, P).transpose(1, 3, 2, 0)
                                    ).reshape(BLOCKS, P, D),
        "v_b": np.ascontiguousarray(np.asarray(peer_v)[0].reshape(P, BLOCKS, D).transpose(1, 0, 2)),
    }
    nc = bacc.Bacc("TRN2", target_bir_lowering=False, num_devices=1)
    aps = {k: nc.dram_tensor(f"in_{k}", a.shape, F32, kind="ExternalInput").ap() for k, a in rows.items()}
    out = nc.dram_tensor("out", (SEQ, D), F32, kind="ExternalOutput").ap()
    hybrid_peer_layer(nc, out=out, **aps)
    r = run_bass_kernel_spmd(nc, [{f"in_{k}": a for k, a in rows.items()}], core_ids=[0])
    return r.results[0]["out"].reshape(1, SEQ, D)
```

```python
from contextlib import ExitStack

import concourse.bass as bass
from concourse import mybir

P = 128
D = 1024
SEQ = 256
DC = D // P
TT = SEQ // P
DIFF_HEADS = 4
MOBA_HEADS = 8
DH = 64
GW = 256
MAPS = 2 * DIFF_HEADS + MOBA_HEADS
PAIRS = MAPS // 2
UNITS = TT * PAIRS
REL_BUCKETS = 32
HEADS = 8
TOPK = 16
HK = HEADS * TOPK
KEYS = 128
LISTS = 2 * HEADS
BLOCKS = 128
HALF = BLOCKS // 2
RAW = 4
PARTS = 4
EXP_AT = 44
TURN_AT = 56
GT = 4
GP = 3
EPS = 1e-6
MASKED = -1e30
LAMBDA_INIT = 0.8 - 0.6
QK_SCALE = DH ** -0.5
TABLE = P - 1 + SEQ
LOG_BUCKETS = [16, 19, 21, 24, 27, 31, 35, 40, 46, 52, 59, 67, 77, 87, 99, 113]
PIECE = DC * D

ALU = mybir.AluOpType
ACT = mybir.ActivationFunctionType
AX = mybir.AxisListType
F32 = mybir.dt.float32
F32R = mybir.dt.float32r
BF16 = mybir.dt.bfloat16
U32 = mybir.dt.uint32


def spread(ap, dim, n):
    shape = list(ap.shape)
    shape.insert(dim, n)
    return ap.unsqueeze(dim).broadcast_to(shape)


def hybrid_peer_layer(nc, x, c_col, rel_t, w_ada, cols, b_row, lam, final_g,
                      w_in, w_out, wq, keys_t, u_t, v_b, out):
    base = (nc.sbuf_base + 31) // 32 * 32
    with ExitStack() as ctx:
        ctx.enter_context(nc.sbuf_tensor("arena", [P, 52900], F32))

        def at(name, word, shape, dt=F32):
            return nc.alloc_sbuf_tensor_at(name, shape, dt, offset=base + 4 * word)

        def sem(name):
            return ctx.enter_context(nc.semaphore(name))

        R = [0, PIECE, 2 * PIECE, 3 * PIECE, 4 * PIECE]
        RAW0, X0, M0, G20, S0 = 40960, 45056, 47104, 51200, 52224
        act = at("act", 0, [P, BLOCKS, SEQ])
        sc1_w = at("sc1_w", R[0], [P, DC, D])
        sh1_w = at("sh1_w", R[2], [P, DC, D])
        g1_w = at("g1_w", R[4], [P, DC, D])
        sc2_w = at("sc2_w", R[0], [P, DC, D])
        sh2_w = at("sh2_w", R[2], [P, DC, D])
        g2_w = at("g2_w", R[1], [P, DC, D])
        place = {"win0": R[4], "win1": R[0], "win2": R[2], "wo": R[4], "wq0": R[0], "wq1": R[2]}
        full = {n: at(n, w, [P, DC, D]) for n, w in place.items()}
        low_of = {n: at(n + "_low", w, [P, DC, D], F32R) for n, w in place.items()}
        high_of = [at("high0", R[3] + 4096, [P, DC, GW], F32R), at("high1", RAW0 + 2048, [P, DC, GW], F32R),
                   at("high2", R[3], [P, DC, GW], F32R), at("high3", R[3] + 2048, [P, DC, GW], F32R)]
        hh = at("hh", R[1], [P, 2, DC, SEQ], F32R)
        logit = at("logit", R[1] + 4096, [P, 2, 2, SEQ])
        prob = at("prob", R[1] + 5120, [P, 2, 2, SEQ])
        probT = at("probT", R[1] + 6144, [P, 2, 4, P])
        g1b = at("g1b", R[1] + 7168, [P, D])
        qk = at("qk", R[3], [P, 2 * PAIRS, SEQ])
        nat = at("nat", R[3] + 4096, [P, TT, D])
        acc = at("acc", R[3] + 6144, [P, 2, D])
        head_junk = at("head_junk", RAW0 + 2048, [P, TT * DIFF_HEADS, P])
        score = at("score", R[3], [P, TT, LISTS, KEYS])
        qT = at("qT", R[3] + 4096, [P, LISTS, SEQ])
        cand = at("cand", R[3] + 4096, [P, HEADS, TOPK, TOPK])
        hit = at("hit", R[3] + 6144, [P, HEADS, TOPK, TOPK])
        top_v = at("top_v", R[2], [P, LISTS, TOPK])
        top_iu = at("top_iu", R[2] + 256, [P, LISTS, TOPK], U32)
        top_i = at("top_i", R[2] + 512, [P, LISTS, TOPK])
        best = at("best", R[2] + 768, [P, HEADS, TOPK])
        best_iu = at("best_iu", R[2] + 896, [P, HEADS, TOPK], U32)
        part_u = at("part_u", R[2] + 1024, [P, 2, HEADS, TOPK], U32)
        part = at("part", R[2] + 1280, [P, 2, HEADS, TOPK])
        chosen = at("chosen", R[2] + 1536, [P, TT, 3, HK])
        gsum = at("gsum", R[2] + 2304, [P, TT, HEADS])
        gate = at("gate", R[2] + 2336, [P, TT, HEADS, TOPK])
        final_gb = at("final_gb", 0, [P, D])
        end_junk = at("end_junk", 1024, [P, TT, D])
        peer = at("peer", 4096, [P, TT, D])
        split = at("split", R[4], [P, 2, 2, D], F32R)
        h2r = at("h2r", R[4] + 4096, [P, 2, DC, SEQ], F32R)
        raw = at("raw", RAW0, [P, RAW, D])
        acc_g2 = at("acc_g2", RAW0, [P, D])
        v = at("v", RAW0, [P, TT, D])
        lam_in = at("lam_in", RAW0, [P, 4 * DH])
        lam_t = at("lam_t", RAW0 + 256, [P, 2, DH])
        rel = at("rel", RAW0 + 512, [MAPS, REL_BUCKETS])
        table = at("table", RAW0 + 1024, [MAPS, TABLE])
        hT = at("hT", RAW0 + 2048, [P, DC, SEQ])
        xs = at("xs", X0, [P, TT, D])
        bias = at("bias", M0, [P, MAPS, SEQ])
        brow2 = at("brow2", M0, [1, D])
        keys = at("keys", M0 + 2048, [P, LISTS, KEYS])
        wsplit = at("wsplit", M0, [P, 2, 2, SEQ], F32R)
        oh1 = at("oh1", M0 + 1024, [P, 2, GT, KEYS], BF16)
        oh2g = at("oh2g", M0 + 1536, [P, 2, GT, GP, HALF], BF16)
        oh2 = at("oh2", M0 + 2304, [P, 2, GT, HALF], BF16)
        chosenT = at("chosenT", M0 + 2560, [P, 3, SEQ])
        part_b = at("part_b", M0 + 3328, [P, SEQ, GP], BF16)
        keys_b = at("keys_b", M0 + 3712, [P, 2, SEQ], BF16)
        iota_b = at("iota_b", M0 + 3968, [P, P], BF16)
        g2b = at("g2b", G20, [P, D])
        brow1 = at("brow1", G20, [1, D])
        ident = at("ident", S0, [P, P])
        iota = at("iota", S0 + 128, [P, P])
        ones = at("ones", S0 + 256, [P, P])
        small = [S0 + 384]

        def sm(name, shape):
            n = 1
            for s in shape[1:]:
                n *= s
            t = at(name, small[0], shape)
            small[0] += (n + 7) // 8 * 8
            return t

        ccol = sm("ccol", [P, DC])
        cact = sm("cact", [P, DC])
        small_cols = sm("small_cols", [P, 6 * DC + 1])
        bcol = small_cols[:, 0:4 * DC].rearrange("p (n c) -> p n c", n=4)
        gain = small_cols[:, 4 * DC:6 * DC].rearrange("p (n c) -> p n c", n=2)
        sub = small_cols[:, 6 * DC:6 * DC + 1]
        a1 = sm("a1", [P, 2, DC])
        a2 = sm("a2", [P, 2, DC])
        sq = sm("sq", [P, 3, TT])
        rstd = sm("rstd", [P, 3, TT])
        sub08 = sm("sub08", [P, 1])
        lsum = sm("lsum", [P, 2])
        lexp = sm("lexp", [P, 2])
        neglam = sm("neglam", [P, 1])
        warm = sm("warm", [P, 3])
        nmax = sm("nmax", [P, UNITS, 2])
        psum_ = sm("psum_", [P, UNITS, 2])
        rsum = sm("rsum", [P, UNITS, 2])
        rlam = sm("rlam", [P, TT * DIFF_HEADS])
        hsq = sm("hsq", [P, TT * DIFF_HEADS])
        hrs = sm("hrs", [P, TT * DIFF_HEADS])
        assert small[0] <= S0 + 676

        banks = ctx.enter_context(nc.psum_tensor("banks", [P, 8, 512], F32))
        bank = [banks[:, n, :] for n in range(8)]
        scratch = nc.dram_tensor("bias_table", [MAPS, TABLE], F32, kind="Internal")

        x_in, c_in, small_in, lam_sem, rel_in, g1row_in, g2row_in, fin_in = map(
            sem, ("x_in", "c_in", "small_in", "lam_sem", "rel_in", "g1row_in", "g2row_in", "fin_in"))
        part_in = [[sem(f"part_in{n}_{e}") for e in range(PARTS)] for n in range(2)]
        win0_in = [sem(f"win0_in{n}") for n in range(D // GW)]
        names = ("win1", "win2", "g1", "sc2", "sh2", "wo", "wq0", "g2", "wq1", "keys")
        loaded = {n: sem(f"loaded_{n}") for n in names}
        raw_full = [sem(f"raw_full{n}") for n in range(RAW)]
        table_built, table_out, bias_in, out_done = map(sem, ("table_built", "table_out", "bias_in", "out_done"))
        const_ready, ones_ready, pool_step = map(sem, ("const_ready", "ones_ready", "pool_step"))
        cact_ready, squared, rooted, normed, lam_exp, lam_ready = map(
            sem, ("cact_ready", "squared", "rooted", "normed", "lam_exp", "lam_ready"))
        v_step = sem("v_step")
        ada_step = sem("ada_step")
        rstd_ready, var_ready, acc_ready, cols_ready, rows_ready, cols_read, rows_read = map(
            sem, ("rstd_ready", "var_ready", "acc_ready", "cols_ready", "rows_ready", "cols_read", "rows_read"))
        xT_ready, hT_ready, h_high, h_split, proj_out = map(
            sem, ("xT_ready", "hT_ready", "h_high", "h_split", "proj_out"))
        group_high, group_low, group_done = map(sem, ("group_high", "group_low", "group_done"))
        scores_ready, logits_ready, max_ready, exp_done, attn_ready = map(
            sem, ("scores_ready", "logits_ready", "max_ready", "exp_done", "attn_ready"))
        pT_ready, pT_out, pv_done, pv_out, head_sq, nat_ready = map(
            sem, ("pT_ready", "pT_out", "pv_done", "pv_out", "head_sq", "nat_ready"))
        mixT_ready, mix_split, x1_ready = map(sem, ("mixT_ready", "mix_split", "x1_ready"))
        x2T_ready, h2T_ready, h2_high, h2_split = map(sem, ("x2T_ready", "h2T_ready", "h2_high", "h2_split"))
        q_out, s_ready, s_out = map(sem, ("q_out", "s_ready", "s_out"))
        gate_max, gate_exp, chosen_ready, cT_ready, cT_out = map(
            sem, ("gate_max", "gate_exp", "chosen_ready", "cT_ready", "cT_out"))
        high_ready, low_ready, block_used, act_ready, act_out = map(
            sem, ("high_ready", "low_ready", "block_used", "act_ready", "act_out"))
        oh2_ready, onehot_ready, gates_ready, gates_out = map(sem, ("oh2_ready", "onehot_ready", "gates_ready", "gates_out"))
        wh_ready, wl_ready, peer_ready, x2_ready, final_ready = map(
            sem, ("wh_ready", "wl_ready", "peer_ready", "x2_ready", "final_ready"))

        block = ctx.enter_context(nc.Block())

        GROUPS = [(n, col) for n in ("win0", "win1", "win2", "wo", "wq0", "wq1") for col in range(0, D, GW)]
        N_IN, N_OUT = 12, 4
        WO, WQ = N_IN, N_IN + N_OUT
        GIVES = [("q", 0), ("q", 2), ("k", 0), ("k", 2), ("v", 0), ("v", GW),
                 ("q", 4), ("q", 6), ("k", 4), ("k", 6), ("v", 512), ("v", 512 + GW)]
        FILL = 6

        def high_slot(w):
            return high_of[w % 2 if w < N_IN else 2 + w % 2]

        ADA = ["sc1", "sh1", "g1", "sc2", "sh2", "g2"]
        ada_w = {"sc1": sc1_w, "sh1": sh1_w, "g1": g1_w, "sc2": sc2_w, "sh2": sh2_w, "g2": g2_w}

        def unit(a):
            return a // 8, a // 4 % TT, a % 4

        def score_banks(a):
            return (3, 4) if a > 8 and a % 2 else (0, 1)

        def pT_bank(a):
            return 5 if a > 8 and a % 2 else 2

        @block.sync
        def _(sp):
            def load(name, dst, src):
                sp.dma_start(dst[:, :, :], src).then_inc(loaded[name], 16)

            sp.dma_start(ccol[:, :], c_col).then_inc(c_in, 16)
            sp.dma_start(xs[:, :, :], x.rearrange("(t p) d -> p t d", p=P)).then_inc(x_in, 16)
            sp.dma_start(small_cols[:, :], cols).then_inc(small_in, 16)
            sp.dma_start(lam_in[:, :], lam.broadcast_to([P, 4 * DH])).then_inc(lam_sem, 16)
            for n, (dst, src) in enumerate(((sc1_w, w_ada[1]), (sh1_w, w_ada[0]))):
                for e in range(PARTS):
                    c = slice(e * DC // PARTS, (e + 1) * DC // PARTS)
                    sp.dma_start(dst[:, c, :], src[:, c, :]).then_inc(part_in[n][e], 16)
            for g in range(D // GW):
                c = slice(g * GW, (g + 1) * GW)
                sp.dma_start(full["win0"][:, :, c], w_in[0][:, :, c]).then_inc(win0_in[g], 16)
            sp.wait_ge(acc_ready, 1)
            load("win1", full["win1"], w_in[1])
            sp.wait_ge(acc_ready, 2)
            load("win2", full["win2"], w_in[2])
            sp.wait_ge(group_done, 4)
            load("g1", g1_w, w_ada[2])
            sp.wait_ge(group_done, 8)
            load("sc2", sc2_w, w_ada[4])
            sp.wait_ge(acc_ready, 3)
            load("wo", full["wo"], w_out)
            sp.wait_ge(group_done, N_IN)
            load("sh2", sh2_w, w_ada[3])
            sp.wait_ge(acc_ready, 4)
            load("wq0", full["wq0"], wq[0])
            sp.wait_ge(logits_ready, UNITS)
            load("keys", keys, keys_t)
            sp.dma_start(brow2[:, :], b_row[1:2, :]).then_inc(g2row_in, 16)
            sp.wait_ge(acc_ready, 5)
            load("wq1", full["wq1"], wq[1])
            sp.wait_ge(x1_ready, N_OUT)
            load("g2", g2_w, w_ada[5])
            sp.wait_ge(rows_ready, 3)
            sp.wait_ge(h2_split, DC // 2)
            for n in range(RAW):
                sp.dma_start(raw[:, n, :], u_t[n]).then_inc(raw_full[n], 16)
            with sp.Fori(1, BLOCKS // RAW) as turn:
                i = turn * RAW
                for s in range(RAW):
                    sp.wait_ge(low_ready, i + (s - RAW + 1))
                    sp.dma_start(raw[:, s, :], u_t[bass.ds(i + s, 1)].rearrange("a p d -> (a p) d")
                                 ).then_inc(raw_full[s], 16)
            with sp.Fori(0, BLOCKS // RAW) as turn:
                i = turn * RAW
                for s in range(RAW):
                    sp.wait_ge(low_ready, i + (BLOCKS + s - RAW + 1))
                    sp.dma_start(raw[:, s, :], v_b[bass.ds(i + s, 1)].rearrange("a p d -> (a p) d")
                                 ).then_inc(raw_full[s], 16)
            sp.wait_ge(wl_ready, BLOCKS)
            sp.wait_ge(wh_ready, BLOCKS)
            sp.dma_start(final_gb[:, :], final_g.broadcast_to([P, D])).then_inc(fin_in, 16)
            for t in range(TT):
                sp.wait_ge(final_ready, t + 1)
                sp.dma_start(out[t * P:(t + 1) * P, :], xs[:, t, :]).then_inc(out_done, 16)
            sp.wait_ge(out_done, 16 * TT)

        @block.gpsimd
        def _(pool):
            pool.dma_start(rel[:, :], rel_t).then_inc(rel_in, 16)
            nc.gpsimd.iota(iota[:, :], [[1, P]], base=0, channel_multiplier=0,
                           allow_small_or_imprecise_dtypes=True).then_inc(const_ready, 1)
            nc.gpsimd.memset(ident[:, :], 0.0).then_inc(pool_step, 1)
            pool.wait_ge(pool_step, 1)
            nc.gpsimd.affine_select(out=ident[:, :], in_=ident[:, :], compare_op=ALU.not_equal, fill=1.0,
                                    base=0, pattern=[[-1, P]], channel_multiplier=1).then_inc(const_ready, 1)
            nc.gpsimd.memset(table[:, 0:P - 1], MASKED).then_inc(table_built, 1)
            pool.wait_ge(rel_in, 16)
            half = REL_BUCKETS // 2
            nc.gpsimd.tensor_copy(table[:, P - 1:P - 1 + half], rel[:, 0:half]).then_inc(table_built, 1)
            for n, lo in enumerate(LOG_BUCKETS):
                hi = (LOG_BUCKETS + [SEQ])[n + 1]
                nc.gpsimd.tensor_copy(table[:, P - 1 + lo:P - 1 + hi],
                                      rel[:, half + n:half + n + 1].broadcast_to([MAPS, hi - lo])
                                      ).then_inc(table_built, 1)
            pool.wait_ge(table_built, 2 + len(LOG_BUCKETS))
            pool.dma_start(scratch.ap(), table[:, :]).then_inc(table_out, 16)
            pool.wait_ge(table_out, 16)
            pool.dma_start(bias[:, :, :], bass.AP(tensor=scratch, offset=0, ap=[[1, P], [TABLE, MAPS], [1, SEQ]])
                           ).then_inc(bias_in, 16)

            for w, (name, col) in enumerate(GROUPS):
                pool.wait_ge(group_high, w + 1)
                for e in range(2):
                    c = slice(col + e * P, col + (e + 1) * P)
                    nc.gpsimd.tensor_tensor(low_of[name][:, :, c], full[name][:, :, c],
                                            high_slot(w)[:, :, e * P:(e + 1) * P].bitcast(F32), ALU.subtract
                                            ).then_inc(group_low, 1)

            def low(n, s):
                pool.wait_ge(high_ready, n + 1)
                nc.gpsimd.tensor_tensor(split[:, s % 2, 1, :], raw[:, s, :],
                                        split[:, s % 2, 0, :].bitcast(F32), ALU.subtract).then_inc(low_ready, 1)

            with pool.Fori(0, (2 * BLOCKS) // RAW) as turn:
                i = turn * RAW
                for s in range(RAW):
                    low(i + s, s)

        @block.scalar
        def _(sc):
            sc.dma_start(brow1[:, :], b_row[0:1, :]).then_inc(g1row_in, 16)
            sc.wait_ge(c_in, 16)
            nc.scalar.activation(cact[:, :], ccol[:, :], ACT.Silu).then_inc(cact_ready, 1)

            def norm_x(n, nth):
                for t in range(TT):
                    if n:
                        sc.wait_ge(x1_ready, N_OUT)
                    nc.scalar.activation(nat[:, t, :], xs[:, t, :], ACT.Square,
                                         accum_out=sq[:, n, t:t + 1]).then_inc(squared, 1)
                sc.wait_ge(var_ready, nth)
                nc.scalar.activation(rstd[:, n, :], sq[:, n, :], ACT.Sqrt).then_inc(rooted, 1)
                sc.wait_ge(rstd_ready, n + 1)
                for t in range(TT):
                    nc.scalar.activation(nat[:, t, :], xs[:, t, :], ACT.Copy,
                                         scale=rstd[:, n, t:t + 1]).then_inc(normed, 1)

            sc.wait_ge(x_in, 16)
            norm_x(0, 1)
            sc.wait_ge(lam_ready, 2)
            nc.scalar.activation(lexp[:, :], lsum[:, :], ACT.Exp).then_inc(lam_exp, 1)
            def warm_table(n, func):
                sc.wait_ge(ones_ready, 1)
                nc.scalar.activation(warm[:, n:n + 1], ones[:, 0:1], func)

            def high_group(w):
                name, col = GROUPS[w]
                sc.wait_ge(win0_in[w] if name == "win0" else loaded[name], 16)
                if w >= 2:
                    sc.wait_ge(group_done, w - 1)
                nc.scalar.activation(high_slot(w)[:, :, :], full[name][:, :, col:col + GW], ACT.Copy
                                     ).then_inc(group_high, 1)

            def high_columns(dst, src_ready, done):
                for b in range(DC // 2):
                    sc.wait_ge(src_ready, 2 * b + 2)
                    nc.scalar.activation(dst[:, 0, 2 * b:2 * b + 2, :], hT[:, 2 * b:2 * b + 2, :], ACT.Copy
                                         ).then_inc(done, 1)

            def proj_copy(g):
                sc.wait_ge(group_done, g + 1)
                kind, n = GIVES[g]
                src = bank[4 - g % 2]
                if kind == "v":
                    if g == 4:
                        sc.wait_ge(lam_ready, 2)
                        sc.wait_ge(table_out, 16)
                    nc.scalar.activation(v[:, :, n:n + GW], src.rearrange("p (t n) -> p t n", t=TT), ACT.Copy
                                         ).then_inc(proj_out, 1)
                else:
                    n += PAIRS if kind == "k" else 0
                    nc.scalar.activation(qk[:, n:n + 2, :].rearrange("p a s -> p (a s)"), src, ACT.Copy,
                                         scale=QK_SCALE if kind == "q" else 1.0).then_inc(proj_out, 1)

            def exps(a):
                nk = (unit(a)[1] + 1) * P
                sc.wait_ge(max_ready, a + 1)
                if a >= 2:
                    sc.wait_ge(pT_ready, a - 1)
                for m in range(2):
                    nc.scalar.activation(prob[:, a % 2, m, 0:nk], logit[:, a % 2, m, 0:nk], ACT.Exp,
                                         bias=nmax[:, a, m:m + 1], accum_out=psum_[:, a, m:m + 1]
                                         ).then_inc(exp_done, 1)

            def pT_copy(a):
                moba, t, _ = unit(a)
                n = (t + 1) * (1 + moba)
                sc.wait_ge(pT_ready, a + 1)
                if a >= 2:
                    sc.wait_ge(pv_done, a - 1)
                nc.scalar.activation(probT[:, a % 2, 0:n, :].rearrange("p n q -> p (n q)"),
                                     bank[pT_bank(a)][:, 0:n * P], ACT.Copy).then_inc(pT_out, 1)

            sc.wait_ge(xT_ready, DC)
            high_group(0)
            high_columns(hh, hT_ready, h_high)
            sc.wait_ge(h_split, DC // 2)
            high_group(1)
            for g in range(FILL):
                proj_copy(g)
                high_group(g + 2)
            for n in range(N_IN - FILL):
                exps(n)
                proj_copy(FILL + n)
                pT_copy(n)
                if FILL + n + 2 < N_IN:
                    high_group(FILL + n + 2)
            exps(N_IN - FILL)
            for a in range(N_IN - FILL, UNITS):
                if a + 1 < UNITS:
                    exps(a + 1)
                pT_copy(a)
                if a == 8:
                    sc.wait_ge(pv_done, 8)
                    nc.scalar.activation(nat[:, :, 0:512], banks[:, 6:8, :], ACT.Copy).then_inc(pv_out, 1)
                    sc.wait_ge(pv_out, 1)
                    for h in range(TT * DIFF_HEADS):
                        t, c0 = h // DIFF_HEADS, h % DIFF_HEADS * P
                        nc.scalar.activation(head_junk[:, h, :], nat[:, t, c0:c0 + P], ACT.Square,
                                             accum_out=hsq[:, h:h + 1]).then_inc(head_sq, 1)
                if a == 12:
                    sc.wait_ge(var_ready, 2)
                    nc.scalar.activation(hrs[:, :], hsq[:, :], ACT.Sqrt).then_inc(rooted, 1)
            sc.wait_ge(scores_ready, UNITS)
            for w in range(WO, WQ + 1):
                high_group(w)
            warm_table(0, ACT.Sqrt)
            norm_x(1, 3)
            high_group(WQ + 1)
            high_columns(h2r, h2T_ready, h2_high)
            for g in range(LISTS // 2):
                sc.wait_ge(group_done, WQ + g + 1)
                nc.scalar.activation(qT[:, 2 * g:2 * g + 2, :].rearrange("p a s -> p (a s)"), bank[4 + g % 4],
                                     ACT.Copy).then_inc(q_out, 1)
                if WQ + g + 2 < len(GROUPS):
                    high_group(WQ + g + 2)
            warm_table(1, ACT.Gelu)
            for g in range(TT * LISTS // 4):
                t, l = g // 4, 4 * (g % 4)
                sc.wait_ge(s_ready, g + 1)
                nc.scalar.activation(score[:, t, l:l + 4, :].rearrange("p l n -> p (l n)"), bank[2 + g % 4],
                                     ACT.Copy).then_inc(s_out, 1)

            def high(n, s, i):
                sc.wait_ge(raw_full[s], i * (16 // RAW) + 16)
                if not (isinstance(n, int) and n < 2):
                    sc.wait_ge(block_used, n - 1)
                nc.scalar.activation(split[:, s % 2, 0, :], raw[:, s, :], ACT.Copy).then_inc(high_ready, 1)

            def gelu(n, s):
                sc.wait_ge(block_used, n + 1)
                nc.scalar.activation(act[:, bass.ds(n, 1), :].rearrange("p a s -> p (a s)"),
                                     bank[4 + s % 2][:, 0:SEQ], ACT.Gelu).then_inc(act_out, 1)

            def whigh(j, s):
                nc.scalar.activation(wsplit[:, s % 2, 0, :], act[:, bass.ds(j, 1), :].rearrange("p a s -> p (a s)"),
                                     ACT.Copy).then_inc(wh_ready, 1)

            def u_blocks(i):
                for s in range(RAW):
                    high(i + s, s, i)
                    if not (isinstance(i, int) and i + s == 0):
                        gelu(i + (s - 1), s - 1)

            u_blocks(0)
            with sc.Fori(1, EXP_AT // RAW) as turn:
                i = turn * RAW
                u_blocks(i)
            for t in range(TT):
                sc.wait_ge(gate_max, t + 1)
                nc.scalar.activation(gate[:, t, :, :], gate[:, t, :, :], ACT.Exp).then_inc(gate_exp, 1)
            u_blocks(EXP_AT)
            with sc.Fori(EXP_AT // RAW + 1, HALF // RAW) as turn:
                i = turn * RAW
                u_blocks(i)
            sc.wait_ge(cT_out, TT)
            with sc.Fori(HALF // RAW, BLOCKS // RAW) as turn:
                i = turn * RAW
                u_blocks(i)
            for s in range(RAW):
                high(BLOCKS + s, s, BLOCKS)
                if s == 0:
                    gelu(BLOCKS - 1, RAW - 1)
                    sc.wait_ge(gates_out, HALF)
                whigh(s, s)
            with sc.Fori(1, HALF // RAW) as turn:
                i = turn * RAW
                for s in range(RAW):
                    high(i + (BLOCKS + s), s, i + BLOCKS)
                    whigh(i + s, s)
            sc.wait_ge(gates_out, 2 * HALF)
            with sc.Fori(HALF // RAW, BLOCKS // RAW) as turn:
                i = turn * RAW
                for s in range(RAW):
                    high(i + (BLOCKS + s), s, i + BLOCKS)
                    whigh(i + s, s)
            warm_table(2, ACT.Sqrt)
            for t in range(TT):
                sc.wait_ge(x2_ready, t + 1)
                nc.scalar.activation(end_junk[:, t, :], xs[:, t, :], ACT.Square,
                                     accum_out=sq[:, 2, t:t + 1]).then_inc(squared, 1)
                sc.wait_ge(var_ready, 4 + t)
                nc.scalar.activation(rstd[:, 2, t:t + 1], sq[:, 2, t:t + 1], ACT.Sqrt).then_inc(rooted, 1)

        @block.tensor
        def _(pe):
            def to_columns(src, done, chunks):
                for c in chunks:
                    for t in range(TT):
                        col = (c % 2) * SEQ + t * P
                        last = nc.tensor.transpose(bank[c // 2][:, col:col + P], src[:, t, c * P:(c + 1) * P],
                                                   ident[:, :])
                    last.then_inc(done, 1)

            def mod_column(k, col, two):
                pe.wait_ge(acc_ready, k + 1)
                for half in range(2):
                    for e in range(DC // 2):
                        c = half * DC // 2 + e
                        last = nc.tensor.matmul(bank[two[half]][:, col + e:col + e + 1],
                                                acc[:, k % 2, c * P:(c + 1) * P], ones[:, 0:1], start=True, stop=True)
                    last.then_inc(cols_ready, 1)

            def mod_row(src, brow, half, dst):
                cols = slice(half * 512, half * 512 + 512)
                nc.tensor.matmul(dst, ones[:, :], src[:, cols], start=True, stop=False)
                return nc.tensor.matmul(dst, ones[0:1, :], brow[0:1, cols], start=False, stop=True)

            def group(w, x, dst, rows, x_split=None):
                name, col = GROUPS[w]
                high, low = high_slot(w), low_of[name]
                pe.wait_ge(group_high, w + 1)
                for e in range(2):
                    out = dst[:, e * 256:(e + 1) * 256]
                    here = slice(e * P, (e + 1) * P)
                    for c in range(DC):
                        if x_split is not None and e == 0 and c % 2 == 0:
                            pe.wait_ge(x_split, c // 2 + 1)
                        for part in range(2):
                            if rows:
                                nc.tensor.matmul(out, x[:, part, c, here], high[:, c, :],
                                                 start=(c == 0 and part == 0), stop=False)
                            else:
                                nc.tensor.matmul(out, high[:, c, here], x[:, part, c, :],
                                                 start=(c == 0 and part == 0), stop=False)
                    pe.wait_ge(group_low, 2 * w + 2 if rows else 2 * w + 1 + e)
                    for c in range(DC):
                        if rows:
                            last = nc.tensor.matmul(out, x[:, 0, c, here], low[:, c, col:col + GW],
                                                    start=False, stop=(c == DC - 1))
                        else:
                            last = nc.tensor.matmul(out, low[:, c, col + e * P:col + (e + 1) * P], x[:, 0, c, :],
                                                    start=False, stop=(c == DC - 1))
                last.then_inc(group_done, 1)

            def proj(g):
                if g >= 2:
                    pe.wait_ge(proj_out, g - 1)
                group(g, hh, bank[4 - g % 2], GIVES[g][0] == "v", h_split if g == 0 else None)

            pe.wait_ge(const_ready, 2)
            pe.wait_ge(normed, TT)
            to_columns(nat, xT_ready, range(DC))
            pe.wait_ge(ones_ready, 1)
            mod_column(0, 0, (6, 7))
            mod_column(1, DC // 2, (6, 7))
            for g in range(FILL):
                proj(g)

            def scores(a):
                moba, t, j = unit(a)
                j += DIFF_HEADS * moba
                nk = (t + 1) * P
                if a > 0:
                    pe.wait_ge(logits_ready, a if a < 9 else a - 1)
                for m in range(2):
                    rows = slice(m * DH, (m + 1) * DH)
                    last = nc.tensor.matmul(bank[score_banks(a)[m]][:, 0:nk], qk[rows, j, t * P:(t + 1) * P],
                                            qk[rows, PAIRS + j, 0:nk], start=True, stop=True)
                last.then_inc(scores_ready, 1)

            def transposes(a):
                moba, t, _ = unit(a)
                if moba:
                    pe.wait_ge(exp_done, 2 * (a + 1))
                else:
                    pe.wait_ge(attn_ready, a + 1)
                if a > 0:
                    pe.wait_ge(pT_out, a if a < 9 else a - 1)
                for m in range(1 + moba):
                    for kb in range(t + 1):
                        n = m * (t + 1) + kb
                        last = nc.tensor.transpose(bank[pT_bank(a)][:, n * P:(n + 1) * P],
                                                   prob[:, a % 2, m, kb * P:(kb + 1) * P], ident[:, :])
                last.then_inc(pT_ready, 1)

            def weigh(a):
                moba, t, j = unit(a)
                pe.wait_ge(pT_out, a + 1)
                if a == 8:
                    pe.wait_ge(pv_out, 1)
                for m in range(1 + moba):
                    w, c0 = (DH, (2 * j + m) * DH) if moba else (P, j * P)
                    v0 = 512 * moba + c0
                    for kb in range(t + 1):
                        last = nc.tensor.matmul(bank[6 + t][:, c0:c0 + w], probT[:, a % 2, m * (t + 1) + kb, :],
                                                v[:, kb, v0:v0 + w], start=(kb == 0), stop=(kb == t))
                last.then_inc(pv_done, 1)

            pe.wait_ge(proj_out, FILL)
            scores(0)
            for a in range(UNITS):
                if a < N_IN - FILL:
                    proj(FILL + a)
                if a in (5, 6):
                    pe.wait_ge(acc_ready, 3)
                    pe.wait_ge(g1row_in, 16)
                    if a == 6:
                        pe.wait_ge(rows_read, 1)
                    mod_row(acc[:, 0, :], brow1, a - 5, bank[5]).then_inc(rows_ready, 1)
                transposes(a)
                if a < 8:
                    if a == 5:
                        pe.wait_ge(proj_out, N_IN)
                    scores(a + 1)
                if 7 <= a < UNITS - 2:
                    if a == 7:
                        pe.wait_ge(rows_read, 2)
                    scores(a + 2)
                if a >= 1:
                    weigh(a - 1)
            weigh(UNITS - 1)

            pe.wait_ge(nat_ready, TT)
            to_columns(nat, mixT_ready, range(DC // 2))
            pe.wait_ge(nat_ready, 2 * TT)
            to_columns(nat, mixT_ready, range(DC // 2, DC))
            for g in range(N_OUT):
                group(WO + g, hh, bank[4 + g], True, mix_split if g == 0 else None)
            mod_column(3, 0, (0, 1))
            mod_column(4, DC // 2, (0, 1))
            pe.wait_ge(normed, 2 * TT)
            pe.wait_ge(cols_read, 4)
            to_columns(nat, x2T_ready, range(DC))

            for g in range(LISTS // 2):
                if g >= 4:
                    pe.wait_ge(q_out, g - 3)
                group(WQ + g, h2r, bank[4 + g % 4], False, h2_split if g == 0 else None)
            pe.wait_ge(acc_ready, 6)
            pe.wait_ge(g2row_in, 16)
            for half in range(2):
                last = mod_row(acc_g2, brow2, half, bank[half])
            last.then_inc(rows_ready, 1)
            pe.wait_ge(loaded["keys"], 16)
            pe.wait_ge(q_out, LISTS // 2)
            for g in range(TT * LISTS // 4):
                t = g // 4
                if g >= 4:
                    pe.wait_ge(s_out, g - 3)
                for e in range(4):
                    l = 4 * (g % 4) + e
                    last = nc.tensor.matmul(bank[2 + g % 4][:, e * P:(e + 1) * P], qT[:, l, t * P:(t + 1) * P],
                                            keys[:, l, :], start=True, stop=True)
                last.then_inc(s_ready, 1)

            def u_block(n, s):
                pe.wait_ge(high_ready, n + 1)
                if not (isinstance(n, int) and n < 2):
                    pe.wait_ge(act_out, n - 1)
                dst = bank[4 + s % 2][:, 0:SEQ]
                for c in range(DC):
                    w = split[:, s % 2, 0, c * P:(c + 1) * P]
                    nc.tensor.matmul(dst, w, h2r[:, 0, c, :], start=(c == 0), stop=False)
                    nc.tensor.matmul(dst, w, h2r[:, 1, c, :], start=False, stop=False)
                pe.wait_ge(low_ready, n + 1)
                for c in range(DC):
                    last = nc.tensor.matmul(dst, split[:, s % 2, 1, c * P:(c + 1) * P], h2r[:, 0, c, :],
                                            start=False, stop=(c == DC - 1))
                last.then_inc(block_used, 1)

            def gates(n, s):
                pe.wait_ge(onehot_ready, n + 1)
                if not (isinstance(n, int) and n < 2):
                    pe.wait_ge(gates_out, n - 1)
                for k in range(GT):
                    for e in range(GP):
                        last = nc.tensor.matmul(bank[6 + s % 2][:, k * HALF:(k + 1) * HALF], oh1[:, s % 2, k, :],
                                                oh2g[:, s % 2, k, e, :], start=(e == 0), stop=(e == GP - 1))
                last.then_inc(gates_ready, 1)

            def v_block(j, s, first=False, last_block=False):
                pe.wait_ge(high_ready, j + (BLOCKS + 1))
                pe.wait_ge(wh_ready, j + 1)
                pe.wait_ge(wl_ready, j + 1)
                for t in range(TT):
                    for e in range(2):
                        for half in range(2):
                            nc.tensor.matmul(bank[2 * t + half][:, :], wsplit[:, s % 2, e, t * P:(t + 1) * P],
                                             split[:, s % 2, 0, half * 512:half * 512 + 512],
                                             start=first and e == 0, stop=False, skip_group_check=True)
                pe.wait_ge(low_ready, j + (BLOCKS + 1))
                for t in range(TT):
                    for half in range(2):
                        last = nc.tensor.matmul(bank[2 * t + half][:, :], wsplit[:, s % 2, 0, t * P:(t + 1) * P],
                                                split[:, s % 2, 1, half * 512:half * 512 + 512],
                                                start=False, stop=last_block, skip_group_check=True)
                last.then_inc(block_used, 1)

            pe.wait_ge(s_out, TT * LISTS // 4)
            for s in range(RAW):
                u_block(s, s)
            with pe.Fori(1, TURN_AT // RAW) as turn:
                i = turn * RAW
                for s in range(RAW):
                    u_block(i + s, s)
            for t in range(TT):
                pe.wait_ge(chosen_ready, 1)
                for k in range(3):
                    last = nc.tensor.transpose(bank[6 + t][:, k * P:(k + 1) * P], chosen[:, t, k, :], ident[:, :])
                last.then_inc(cT_ready, 1)
            with pe.Fori(TURN_AT // RAW, HALF // RAW) as turn:
                i = turn * RAW
                for s in range(RAW):
                    u_block(i + s, s)
            pe.wait_ge(cT_out, TT)
            for s in range(RAW):
                u_block(HALF + s, s)
                gates(s, s)
            with pe.Fori(1, HALF // RAW) as turn:
                i = turn * RAW
                for s in range(RAW):
                    u_block(i + (HALF + s), s)
                    gates(i + s, s)
            pe.wait_ge(rows_read, 3)
            for s in range(RAW):
                v_block(s, s, first=(s == 0))
                gates(HALF + s, s)
            with pe.Fori(1, HALF // RAW) as turn:
                i = turn * RAW
                for s in range(RAW):
                    v_block(i + s, s)
                    gates(i + (HALF + s), s)
            with pe.Fori(HALF // RAW, (BLOCKS - RAW) // RAW) as turn:
                i = turn * RAW
                for s in range(RAW):
                    v_block(i + s, s)
            for s in range(RAW):
                v_block(BLOCKS - RAW + s, s, last_block=(s == RAW - 1))
            pe.wait_ge(block_used, 2 * BLOCKS)
            pe.nop().then_inc(peer_ready, 1)

        @block.vector
        def _(ve):
            steps = [0]
            ada_steps = [0]

            def link(ins):
                steps[0] += 1
                ins.then_inc(v_step, 1)
                ve.wait_ge(v_step, steps[0])

            def ada(k, chunks):
                w = ada_w[ADA[k]]
                dst = acc_g2[:, :] if k == 5 else acc[:, k % 2, :]
                for c in chunks:
                    if c == 0:
                        ve.wait_ge(loaded[ADA[k]] if k >= 2 else part_in[k][0], 16)
                        if k == 2 or k == 3:
                            ve.wait_ge(cols_ready, 2 * (k - 1))
                        if k == 4:
                            ve.wait_ge(rows_ready, 2)
                        ins = nc.vector.tensor_scalar(dst, w[:, 0, :], cact[:, 0:1], None, ALU.mult)
                    else:
                        if k < 2 and c % (DC // PARTS) == 0:
                            ve.wait_ge(part_in[k][c * PARTS // DC], 16)
                        ve.wait_ge(ada_step, ada_steps[0])
                        ins = nc.vector.scalar_tensor_tensor(out=dst, in0=w[:, c, :], scalar=cact[:, c:c + 1],
                                                             in1=dst, op0=ALU.mult, op1=ALU.add)
                    if c < DC - 1:
                        ins.then_inc(ada_step, 1)
                        ada_steps[0] += 1
                    else:
                        ins.then_inc(acc_ready, 1)

            def root(n, nth, count):
                ve.wait_ge(squared, count)
                nc.vector.tensor_scalar(sq[:, n, :], sq[:, n, :], 1.0 / D, EPS, ALU.mult, ALU.add
                                        ).then_inc(var_ready, 1)
                ve.wait_ge(rooted, nth)
                nc.vector.reciprocal(rstd[:, n, :], rstd[:, n, :]).then_inc(rstd_ready, 1)

            def modulate(a, n, half, b):
                cols = bank[b][:, 0:DC].rearrange("p (a c) -> p a c", a=2)
                c = slice(half * DC // 2, (half + 1) * DC // 2)
                ve.wait_ge(cols_ready, 4 * n + 3 + half)
                nc.vector.tensor_tensor(a[:, :, c], cols, bcol[:, 2 * n:2 * n + 2, c], ALU.add
                                        ).then_inc(cols_read, 1)
                ve.wait_ge(cols_read, 2 * n + half + 1)
                link(nc.vector.scalar_tensor_tensor(out=a[:, 0, c], in0=a[:, 0, c], scalar=1.0, in1=gain[:, n, c],
                                                    op0=ALU.add, op1=ALU.mult))

            def split_columns(dst, a, src_ready, dst_ready, high, done):
                for b in range(DC // 2):
                    if a is a1 and b % 2 == 0:
                        modulate(a1, 0, b // 2, 6 + b // 2)
                    ve.wait_ge(src_ready, 2 * b + 2)
                    for c in (2 * b, 2 * b + 1):
                        nc.vector.tensor_scalar(hT[:, c, :], bank[b][:, (c % 2) * SEQ:(c % 2 + 1) * SEQ],
                                                a[:, 0, c:c + 1], a[:, 1, c:c + 1], ALU.mult, ALU.add
                                                ).then_inc(dst_ready, 1)
                    if b:
                        rest(dst, b - 1, dst_ready, high, done)
                rest(dst, DC // 2 - 1, dst_ready, high, done)

            def rest(dst, b, src_ready, high, done):
                two = slice(2 * b, 2 * b + 2)
                ve.wait_ge(src_ready, 2 * b + 2)
                ve.wait_ge(high, b + 1)
                nc.vector.tensor_tensor(dst[:, 1, two, :], hT[:, two, :], dst[:, 0, two, :].bitcast(F32),
                                        ALU.subtract).then_inc(done, 1)

            nc.vector.memset(ones[:, :], 1.0).then_inc(ones_ready, 1)
            ve.wait_ge(lam_sem, 16)
            for n in range(2):
                nc.vector.tensor_tensor_reduce(out=lam_t[:, n, :], in0=lam_in[:, 2 * n * DH:(2 * n + 1) * DH],
                                               in1=lam_in[:, (2 * n + 1) * DH:(2 * n + 2) * DH], scale=1.0,
                                               scalar=0.0, op0=ALU.mult, op1=ALU.add,
                                               accum_out=lsum[:, n:n + 1]).then_inc(lam_ready, 1)
            root(0, 1, TT)
            ve.wait_ge(cact_ready, 1)
            ada(0, range(DC))
            ada(1, range(DC))
            ve.wait_ge(lam_exp, 1)
            link(nc.vector.scalar_tensor_tensor(out=neglam[:, :], in0=lexp[:, 1:2], scalar=-LAMBDA_INIT,
                                                in1=lexp[:, 0:1], op0=ALU.add, op1=ALU.subtract))
            ve.wait_ge(small_in, 16)
            nc.vector.tensor_scalar(sub08[:, :], sub, 1.0 - LAMBDA_INIT, None, ALU.mult)
            split_columns(hh, a1, xT_ready, hT_ready, h_high, h_split)

            def logits(a):
                moba, t, j = unit(a)
                nk = (t + 1) * P
                m0 = 2 * (j + DIFF_HEADS * moba)
                b0 = score_banks(a)[0]
                ve.wait_ge(scores_ready, a + 1)
                if a >= 2:
                    ve.wait_ge(exp_done, 2 * (a - 1))
                nc.vector.tensor_tensor(logit[:, a % 2, :, 0:nk], banks[:, b0:b0 + 2, 0:nk],
                                        bias[:, m0:m0 + 2, 0:nk][:, :, ::-1], ALU.add).then_inc(logits_ready, 1)
                ve.wait_ge(logits_ready, a + 1)
                nc.vector.tensor_reduce(nmax[:, a, :], logit[:, a % 2, :, 0:nk], AX.X, ALU.max,
                                        negate=True).then_inc(max_ready, 1)

            def combine(a):
                _, t, j = unit(a)
                nk = (t + 1) * P
                ve.wait_ge(exp_done, 2 * (a + 1))
                link(nc.vector.reciprocal(rsum[:, a, :], psum_[:, a, :]))
                link(nc.vector.tensor_scalar(rlam[:, a:a + 1], rsum[:, a, 1:2], neglam[:, 0:1], None, ALU.mult))
                link(nc.vector.tensor_scalar(prob[:, a % 2, 1, 0:nk], prob[:, a % 2, 1, 0:nk], rlam[:, a:a + 1],
                                             None, ALU.mult))
                nc.vector.scalar_tensor_tensor(out=prob[:, a % 2, 0, 0:nk], in0=prob[:, a % 2, 0, 0:nk],
                                               scalar=rsum[:, a, 0:1], in1=prob[:, a % 2, 1, 0:nk],
                                               op0=ALU.mult, op1=ALU.add).then_inc(attn_ready, 1)

            def row_copy(n, src, dst):
                ve.wait_ge(rows_ready, n)
                nc.vector.tensor_copy(dst, src).then_inc(rows_read, 1)

            ve.wait_ge(bias_in, 16)
            for a in range(8):
                logits(a)
                combine(a)
                if 1 <= a <= 4:
                    ada(2, range(2 * a - 2, 2 * a))
                if a in (5, 6):
                    row_copy(a - 4, bank[5], g1b[:, (a - 5) * 512:(a - 4) * 512])
            logits(8)
            for a in range(8, UNITS):
                if a + 1 < UNITS:
                    logits(a + 1)
                if a < 12:
                    ada(3, range(2 * a - 16, 2 * a - 14))
                if a == 11:
                    ve.wait_ge(head_sq, TT * DIFF_HEADS)
                    nc.vector.tensor_scalar(hsq[:, :], hsq[:, :], 1.0 / P, EPS, ALU.mult, ALU.add
                                            ).then_inc(var_ready, 1)
                if a == 14:
                    ve.wait_ge(rooted, 2)
                    link(nc.vector.reciprocal(hrs[:, :], hrs[:, :]))
                    for t in range(TT):
                        heads = nat[:, t, 0:512].rearrange("p (h d) -> p h d", d=P)
                        nc.vector.tensor_tensor(heads, heads,
                                                spread(hrs[:, t * DIFF_HEADS:(t + 1) * DIFF_HEADS], 2, P), ALU.mult
                                                ).then_inc(nat_ready, 1)

            ve.wait_ge(exp_done, 2 * UNITS)
            link(nc.vector.reciprocal(rsum[:, 8:UNITS, :], psum_[:, 8:UNITS, :]))
            for t in range(TT):
                ve.wait_ge(pv_done, 12 + 4 * t)
                inv = rsum[:, 8 + 4 * t:12 + 4 * t, :].rearrange("p j m -> p (j m)")
                nc.vector.tensor_tensor(nat[:, t, 512:D].rearrange("p (h d) -> p h d", d=DH),
                                        bank[6 + t].rearrange("p (h d) -> p h d", d=DH),
                                        spread(inv, 2, DH), ALU.mult).then_inc(nat_ready, 1)
            for b in range(DC // 2):
                src = bank[b].rearrange("p (c s) -> p c s", c=2)
                two = slice(2 * b, 2 * b + 2)
                ve.wait_ge(mixT_ready, 2 * b + 2)
                if 2 * b < DIFF_HEADS:
                    link(nc.vector.tensor_scalar(hh[:, 0, two, :], src, sub08[:, 0:1], None, ALU.mult))
                    nc.vector.scalar_tensor_tensor(out=hh[:, 1, two, :], in0=src, scalar=sub08[:, 0:1],
                                                   in1=hh[:, 0, two, :].bitcast(F32), op0=ALU.mult,
                                                   op1=ALU.subtract).then_inc(mix_split, 1)
                else:
                    link(nc.vector.tensor_copy(hh[:, 0, two, :], src))
                    nc.vector.tensor_tensor(hh[:, 1, two, :], src, hh[:, 0, two, :].bitcast(F32),
                                            ALU.subtract).then_inc(mix_split, 1)
            ada(4, range(DC))
            for g in range(N_OUT):
                cols = slice(g * GW, (g + 1) * GW)
                ve.wait_ge(group_done, WO + g + 1)
                link(nc.vector.tensor_tensor(nat[:, :, cols], bank[4 + g].rearrange("p (t n) -> p t n", t=TT),
                                             spread(g1b[:, cols], 1, TT), ALU.mult))
                nc.vector.tensor_tensor(xs[:, :, cols], xs[:, :, cols], nat[:, :, cols], ALU.add
                                        ).then_inc(x1_ready, 1)
            for half in range(2):
                modulate(a2, 1, half, half)
            root(1, 3, 2 * TT)
            split_columns(h2r, a2, x2T_ready, h2T_ready, h2_high, h2_split)
            ada(5, range(DC))
            ve.wait_ge(rows_ready, 3)
            nc.vector.tensor_copy(g2b[:, :], banks[:, 0:2, :].rearrange("p b n -> p (b n)")).then_inc(rows_read, 1)

            def top16(vals, idx, src, n):
                for k in range(0, TOPK, 8):
                    for l in range(n):
                        last = nc.vector.max(vals[:, l, k:k + 8], src(l))
                    link(last)
                    for l in range(n):
                        last = nc.vector.max_index(idx[:, l, k:k + 8], vals[:, l, k:k + 8], src(l))
                    link(last)
                    if k + 8 < TOPK:
                        for l in range(n):
                            last = nc.vector.match_replace(src(l), vals[:, l, k:k + 8], src(l), -3.0e38)
                        link(last)

            for t in range(TT):
                ve.wait_ge(s_out, (t + 1) * LISTS // 4)
                if t == 0:
                    ve.wait_ge(s_ready, TT * LISTS // 4)
                top16(top_v, top_iu, lambda l: score[:, t, l, :], LISTS)
                link(nc.vector.tensor_copy(top_i[:, :, :], top_iu[:, :, :]))
                halves_v = top_v[:, :, :].rearrange("p (h two) k -> p two h k", two=2)
                halves_i = top_i[:, :, :].rearrange("p (h two) k -> p two h k", two=2)
                link(nc.vector.tensor_tensor(cand[:, :, :, :], spread(halves_v[:, 0], 3, TOPK),
                                             spread(halves_v[:, 1], 2, TOPK), ALU.add))
                top16(best, best_iu, lambda h: cand[:, h, :, :].rearrange("p a b -> p (a b)"), HEADS)
                nc.vector.tensor_tensor(gate[:, t, :, :], best[:, :, :],
                                        best[:, :, 0:1].broadcast_to([P, HEADS, TOPK]), ALU.subtract
                                        ).then_inc(gate_max, 1)
                nc.vector.tensor_scalar(part_u[:, 0, :, :], best_iu[:, :, :], 4, None, ALU.logical_shift_right)
                link(nc.vector.tensor_scalar(part_u[:, 1, :, :], best_iu[:, :, :], TOPK - 1, None,
                                             ALU.bitwise_and))
                link(nc.vector.tensor_copy(part[:, :, :, :], part_u[:, :, :, :]))
                for half in range(2):
                    place = spread(spread(iota[:, 0:TOPK], 1, TOPK), 1, HEADS)
                    link(nc.vector.tensor_tensor(hit[:, :, :, :], spread(part[:, half], 3, TOPK), place,
                                                 ALU.is_equal))
                    link(nc.vector.tensor_tensor(hit[:, :, :, :], hit[:, :, :, :],
                                                 spread(halves_i[:, half], 2, TOPK), ALU.mult))
                    link(nc.vector.tensor_reduce(chosen[:, t, half, :], hit[:, :, :, :], AX.X, ALU.add))
            ve.wait_ge(gate_exp, TT)
            link(nc.vector.tensor_reduce(gsum[:, :, :], gate[:, :, :, :], AX.X, ALU.add))
            link(nc.vector.reciprocal(gsum[:, :, :], gsum[:, :, :]))
            nc.vector.tensor_tensor(chosen[:, :, 2, :].rearrange("p t (h k) -> p t h k", k=TOPK),
                                    gate[:, :, :, :], spread(gsum[:, :, :], 3, TOPK), ALU.mult
                                    ).then_inc(chosen_ready, 1)
            for t in range(TT):
                ve.wait_ge(cT_ready, t + 1)
                nc.vector.tensor_copy(chosenT[:, :, t * P:(t + 1) * P],
                                      bank[6 + t][:, 0:3 * P].rearrange("p (k q) -> p k q", k=3)
                                      ).then_inc(cT_out, 1)
            ve.wait_ge(cT_out, TT)
            nc.vector.tensor_copy(iota_b[:, :], iota[:, :])
            link(nc.vector.tensor_copy(keys_b[:, :, :], chosenT[:, 0:2, :]))
            for e in range(GP):
                link(nc.vector.tensor_copy(part_b[:, :, e], chosenT[:, 2, :]))
                if e < GP - 1:
                    link(nc.vector.tensor_tensor(chosenT[:, 2, :], chosenT[:, 2, :], part_b[:, :, e],
                                                 ALU.subtract))

            def onehots(q, s, half):
                n = q + half * HALF
                if not (isinstance(n, int) and n < 2):
                    ve.wait_ge(gates_ready, n - 1)
                toks = bass.ds(q * GT, GT)
                nc.vector.tensor_tensor(oh2[:, s % 2, :, :], spread(iota_b[:, half * HALF:(half + 1) * HALF], 1, GT),
                                        spread(keys_b[:, 1, toks], 2, HALF), ALU.is_equal).then_inc(oh2_ready, 1)
                nc.vector.tensor_tensor(oh1[:, s % 2, :, :], spread(iota_b[:, :], 1, GT),
                                        spread(keys_b[:, 0, toks], 2, KEYS), ALU.is_equal)
                ve.wait_ge(oh2_ready, n + 1)
                nc.vector.tensor_tensor(oh2g[:, s % 2, :, :, :], spread(oh2[:, s % 2, :, :], 2, GP),
                                        spread(part_b[:, toks, :], 3, HALF), ALU.mult).then_inc(onehot_ready, 1)

            def gate_acts(q, s, half):
                ve.wait_ge(gates_ready, q + (half * HALF + 1))
                dst = act[:, half * HALF:(half + 1) * HALF, bass.ds(q * GT, GT)]
                nc.vector.tensor_tensor(dst, bank[6 + s % 2][:, 0:GT * HALF].rearrange("p (k j) -> p j k", k=GT),
                                        dst, ALU.mult).then_inc(gates_out, 1)

            def wlow(j, s):
                ve.wait_ge(wh_ready, j + 1)
                nc.vector.tensor_tensor(wsplit[:, s % 2, 1, :], act[:, bass.ds(j, 1), :].rearrange("p a s -> p (a s)"),
                                        wsplit[:, s % 2, 0, :].bitcast(F32), ALU.subtract).then_inc(wl_ready, 1)

            for s in range(RAW):
                onehots(s, s, 0)
                if s == 1:
                    ve.wait_ge(act_out, HALF)
                if s:
                    gate_acts(s - 1, s - 1, 0)
            with ve.Fori(1, HALF // RAW) as turn:
                q = turn * RAW
                for s in range(RAW):
                    onehots(q + s, s, 0)
                    gate_acts(q + (s - 1), s - 1, 0)
            gate_acts(HALF - 1, RAW - 1, 0)
            ve.wait_ge(gates_out, HALF)
            ve.wait_ge(act_out, BLOCKS)
            for s in range(RAW):
                wlow(s, s)
                onehots(s, s, 1)
                if s:
                    gate_acts(s - 1, s - 1, 1)
            with ve.Fori(1, HALF // RAW) as turn:
                q = turn * RAW
                for s in range(RAW):
                    wlow(q + s, s)
                    onehots(q + s, s, 1)
                    gate_acts(q + (s - 1), s - 1, 1)
            gate_acts(HALF - 1, RAW - 1, 1)
            ve.wait_ge(gates_out, 2 * HALF)
            with ve.Fori(HALF // RAW, BLOCKS // RAW) as turn:
                j = turn * RAW
                for s in range(RAW):
                    wlow(j + s, s)

            ve.wait_ge(peer_ready, 1)
            ve.wait_ge(wl_ready, BLOCKS)
            for t in range(TT):
                link(nc.vector.tensor_tensor(peer[:, t, :], banks[:, 2 * t:2 * t + 2, :].rearrange("p b n -> p (b n)"),
                                             g2b[:, :], ALU.mult))
                nc.vector.tensor_tensor(xs[:, t, :], xs[:, t, :], peer[:, t, :], ALU.add).then_inc(x2_ready, 1)
            ve.wait_ge(fin_in, 16)
            for t in range(TT):
                ve.wait_ge(squared, 2 * TT + t + 1)
                nc.vector.tensor_scalar(sq[:, 2, t:t + 1], sq[:, 2, t:t + 1], 1.0 / D, EPS, ALU.mult, ALU.add
                                        ).then_inc(var_ready, 1)
                ve.wait_ge(rooted, 4 + t)
                link(nc.vector.reciprocal(rstd[:, 2, t:t + 1], rstd[:, 2, t:t + 1]))
                nc.vector.scalar_tensor_tensor(out=xs[:, t, :], in0=xs[:, t, :], scalar=rstd[:, 2, t:t + 1],
                                               in1=final_gb[:, :], op0=ALU.mult, op1=ALU.mult
                                               ).then_inc(final_ready, 1)


def kernel(x, c, rel_bias, w_ada, b_ada, norm1_g, w_in, diff_lambda, diff_subln_g,
           w_out, norm2_g, peer_wq, peer_keys, peer_u, peer_v, final_g):
    import numpy as np
    import concourse.bacc as bacc
    from concourse.bass_utils import run_bass_kernel_spmd

    def wide(w):
        w = np.asarray(w)
        return np.ascontiguousarray(w.reshape(DC, P, -1, D).transpose(2, 1, 0, 3))

    def column(w):
        w = np.asarray(w)
        return np.ascontiguousarray(np.moveaxis(w.reshape(w.shape[:-1] + (DC, P)), -1, 0))

    maps = [m * DIFF_HEADS + j for j in range(DIFF_HEADS) for m in range(2)] + list(range(8, MAPS))
    b = np.asarray(b_ada)[0].reshape(6, D)
    rows = {
        "x": np.asarray(x)[0],
        "c_col": column(np.asarray(c)[0]),
        "rel_t": np.ascontiguousarray(np.asarray(rel_bias)[:, maps].T),
        "w_ada": wide(w_ada[0]),
        "b_row": np.ascontiguousarray(b[[2, 5]]),
        "cols": np.concatenate([column(b[[1, 0, 4, 3]]).reshape(P, -1), column(np.asarray(norm1_g)[0]),
                                column(np.asarray(norm2_g)[0]), np.asarray(diff_subln_g)[0].reshape(P, 1)], 1),
        "lam": np.ascontiguousarray(np.asarray(diff_lambda).reshape(1, 4 * DH)),
        "final_g": np.ascontiguousarray(np.asarray(final_g).reshape(1, D)),
        "w_in": wide(w_in[0]),
        "w_out": wide(w_out[0])[0],
        "wq": wide(peer_wq[0]),
        "keys_t": np.ascontiguousarray(np.asarray(peer_keys)[0].reshape(LISTS, KEYS, P).transpose(2, 0, 1)),
        "u_t": np.ascontiguousarray(np.asarray(peer_u)[0].reshape(P, BLOCKS, DC, P).transpose(1, 3, 2, 0)
                                    ).reshape(BLOCKS, P, D),
        "v_b": np.ascontiguousarray(np.asarray(peer_v)[0].reshape(P, BLOCKS, D).transpose(1, 0, 2)),
    }
    nc = bacc.Bacc("TRN2", target_bir_lowering=False, num_devices=1)
    aps = {k: nc.dram_tensor(f"in_{k}", a.shape, F32, kind="ExternalInput").ap() for k, a in rows.items()}
    out = nc.dram_tensor("out", (SEQ, D), F32, kind="ExternalOutput").ap()
    hybrid_peer_layer(nc, out=out, **aps)
    r = run_bass_kernel_spmd(nc, [{f"in_{k}": a for k, a in rows.items()}], core_ids=[0])
    return r.results[0]["out"].reshape(1, SEQ, D)
```

```python
from contextlib import ExitStack

import concourse.bass as bass
from concourse import mybir

P = 128
D = 1024
SEQ = 256
DC = D // P
TT = SEQ // P
DIFF_HEADS = 4
MOBA_HEADS = 8
DH = 64
GW = 256
MAPS = 2 * DIFF_HEADS + MOBA_HEADS
PAIRS = MAPS // 2
UNITS = TT * PAIRS
REL_BUCKETS = 32
HEADS = 8
TOPK = 16
HK = HEADS * TOPK
KEYS = 128
LISTS = 2 * HEADS
BLOCKS = 128
HALF = BLOCKS // 2
RAW = 4
TURN = 8
PARTS = 4
LATE = 13
EXP_AT = 44
TURN_AT = 56
GT = 8
NG = SEQ // GT
GP = 2
GATE_SCALE = 2.0 ** 14
EPS = 1e-6
MASKED = -1e30
LAMBDA_INIT = 0.8 - 0.6
QK_SCALE = DH ** -0.5
TABLE = P - 1 + SEQ
LOG_BUCKETS = [16, 19, 21, 24, 27, 31, 35, 40, 46, 52, 59, 67, 77, 87, 99, 113]
PIECE = DC * D

ALU = mybir.AluOpType
ACT = mybir.ActivationFunctionType
AX = mybir.AxisListType
F32 = mybir.dt.float32
F32R = mybir.dt.float32r
F16 = mybir.dt.float16
U32 = mybir.dt.uint32


def spread(ap, dim, n):
    shape = list(ap.shape)
    shape.insert(dim, n)
    return ap.unsqueeze(dim).broadcast_to(shape)


def hybrid_peer_layer(nc, x, c_col, rel_t, w_ada, cols, b_row, lam, final_g,
                      w_in, w_out, wq, keys_t, u_t, v_b, out):
    base = (nc.sbuf_base + 31) // 32 * 32
    with ExitStack() as ctx:
        ctx.enter_context(nc.sbuf_tensor("arena", [P, 52900], F32))

        def at(name, word, shape, dt=F32):
            return nc.alloc_sbuf_tensor_at(name, shape, dt, offset=base + 4 * word)

        def sem(name):
            return ctx.enter_context(nc.semaphore(name))

        R = [0, PIECE, 2 * PIECE, 3 * PIECE, 4 * PIECE]
        RAW0, X0, M0, G20, S0 = 40960, 45056, 47104, 51200, 52224
        act = at("act", 0, [P, BLOCKS, SEQ])
        sc1_w = at("sc1_w", R[0], [P, DC, D])
        sh1_w = at("sh1_w", R[2], [P, DC, D])
        g1_w = at("g1_w", R[4], [P, DC, D])
        sc2_w = at("sc2_w", R[0], [P, DC, D])
        sh2_w = at("sh2_w", R[2], [P, DC, D])
        g2_w = at("g2_w", R[1], [P, DC, D])
        place = {"win0": R[4], "win1": R[0], "win2": R[2], "wo": R[4], "wq0": R[0], "wq1": R[2]}
        full = {n: at(n, w, [P, DC, D]) for n, w in place.items()}
        low_of = {n: at(n + "_low", w, [P, DC, D], F32R) for n, w in place.items()}
        high_of = [at("high0", R[3] + 4096, [P, DC, GW], F32R), at("high1", RAW0 + 2048, [P, DC, GW], F32R),
                   at("high2", R[3], [P, DC, GW], F32R), at("high3", R[3] + 2048, [P, DC, GW], F32R)]
        hh = at("hh", R[1], [P, 2, DC, SEQ], F32R)
        logit = at("logit", R[1] + 4096, [P, 2, 2, SEQ])
        prob = at("prob", R[1] + 5120, [P, 2, 2, SEQ])
        probT = at("probT", R[1] + 6144, [P, 2, 4, P])
        g1b = at("g1b", R[1] + 7168, [P, D])
        qk = at("qk", R[3], [P, 2 * PAIRS, SEQ])
        nat = at("nat", R[3] + 4096, [P, TT, D])
        acc = at("acc", R[3] + 6144, [P, 2, D])
        score = at("score", R[3], [P, TT, LISTS, KEYS])
        qT = at("qT", R[3] + 4096, [P, LISTS, SEQ])
        cand = at("cand", R[3] + 4096, [P, HEADS, TOPK, TOPK])
        hit = at("hit", R[3] + 6144, [P, HEADS, TOPK, TOPK])
        top_v = at("top_v", R[2], [P, LISTS, TOPK])
        top_iu = at("top_iu", R[2] + 256, [P, LISTS, TOPK], U32)
        top_i = at("top_i", R[2] + 512, [P, LISTS, TOPK])
        best = at("best", R[2] + 768, [P, HEADS, TOPK])
        best_iu = at("best_iu", R[2] + 896, [P, HEADS, TOPK], U32)
        part_u = at("part_u", R[2] + 1024, [P, 2, HEADS, TOPK], U32)
        part = at("part", R[2] + 1280, [P, 2, HEADS, TOPK])
        chosen = at("chosen", R[2] + 1536, [P, TT, 3, HK])
        gsum = at("gsum", R[2] + 2304, [P, TT, HEADS])
        gate = at("gate", R[2] + 2336, [P, TT, HEADS, TOPK])
        final_gb = at("final_gb", 0, [P, D])
        end_junk = at("end_junk", 1024, [P, TT, D])
        peer = at("peer", 4096, [P, TT, D])
        split = at("split", R[4], [P, 2, 2, D], F32R)
        h2r = at("h2r", R[4] + 4096, [P, 2, DC, SEQ], F32R)
        raw = at("raw", RAW0, [P, RAW, D])
        acc_g2 = at("acc_g2", RAW0, [P, D])
        v = at("v", RAW0, [P, TT, D])
        lam_in = at("lam_in", RAW0, [P, 4 * DH])
        lam_t = at("lam_t", RAW0 + 256, [P, 2, DH])
        rel = at("rel", RAW0 + 512, [MAPS, REL_BUCKETS])
        table = at("table", RAW0 + 1024, [MAPS, TABLE])
        diag = at("diag", RAW0 + 1536, [P, TT, P])
        hT = at("hT", RAW0 + 2048, [P, DC, SEQ])
        xs = at("xs", X0, [P, TT, D])
        bias = at("bias", M0, [P, MAPS, SEQ])
        diff_out = at("diff_out", M0, [P, TT, 512])
        head_junk = at("head_junk", M0 + 1024, [P, TT * DIFF_HEADS, P])
        brow2 = at("brow2", M0, [1, D])
        keys = at("keys", M0 + 2048, [P, LISTS, KEYS])
        wsplit = at("wsplit", M0, [P, 2, 2, SEQ], F32R)
        chosenT = at("chosenT", M0 + 1024, [P, 3, SEQ])
        oh1 = at("oh1", M0 + 1024, [P, 2, GT, KEYS], F16)
        oh2g = at("oh2g", M0 + 2048, [P, 2, GT, GP, HALF], F16)
        oh2 = at("oh2", M0 + 3072, [P, 2, GT, HALF], F16)
        part_h = at("part_h", M0 + 3584, [P, SEQ, GP], F16)
        keys_h = at("keys_h", M0 + 3840, [P, 2, SEQ], F16)
        iota_h = at("iota_h", S0 + 320, [P, P], F16)
        g2b = at("g2b", G20, [P, D])
        brow1 = at("brow1", G20, [1, D])
        ident = at("ident", S0, [P, P])
        iota = at("iota", S0 + 128, [P, P])
        ones = at("ones", S0 + 256, [P, P])
        small = [S0 + 384]

        def sm(name, shape):
            n = 1
            for s in shape[1:]:
                n *= s
            t = at(name, small[0], shape)
            small[0] += (n + 7) // 8 * 8
            return t

        ccol = sm("ccol", [P, DC])
        cact = sm("cact", [P, DC])
        small_cols = sm("small_cols", [P, 6 * DC + 1])
        bcol = small_cols[:, 0:4 * DC].rearrange("p (n c) -> p n c", n=4)
        gain = small_cols[:, 4 * DC:6 * DC].rearrange("p (n c) -> p n c", n=2)
        sub = small_cols[:, 6 * DC:6 * DC + 1]
        a1 = sm("a1", [P, 2, DC])
        a2 = sm("a2", [P, 2, DC])
        sq = sm("sq", [P, 3, TT])
        rstd = sm("rstd", [P, 3, TT])
        sq_cols = sm("sq_cols", [P, TT, D // GW])
        sub08 = sm("sub08", [P, 1])
        lsum = sm("lsum", [P, 2])
        lexp = sm("lexp", [P, 2])
        neglam = sm("neglam", [P, 1])
        warm = sm("warm", [P, 2])
        nmax = sm("nmax", [P, UNITS, 2])
        psum_ = sm("psum_", [P, UNITS, 2])
        rsum = sm("rsum", [P, UNITS, 2])
        rlam = sm("rlam", [P, TT * DIFF_HEADS])
        hsq = sm("hsq", [P, TT * DIFF_HEADS])
        hrs = sm("hrs", [P, TT * DIFF_HEADS])
        assert small[0] <= S0 + 676

        banks = ctx.enter_context(nc.psum_tensor("banks", [P, 8, 512], F32))
        bank = [banks[:, n, :] for n in range(8)]
        scratch = nc.dram_tensor("bias_table", [MAPS, TABLE], F32, kind="Internal")

        x_in, c_in, small_in, lam_sem, rel_in, g1row_in, g2row_in, fin_in = map(
            sem, ("x_in", "c_in", "small_in", "lam_sem", "rel_in", "g1row_in", "g2row_in", "fin_in"))
        part_in = [[sem(f"part_in{n}_{e}") for e in range(PARTS)] for n in range(2)]
        win_in = {n: [sem(f"{n}_in{g}") for g in range(D // GW)] for n in ("win0", "win1")}
        names = ("win2", "g1", "sc2", "sh2", "wo", "wq0", "g2", "wq1", "keys")
        loaded = {n: sem(f"loaded_{n}") for n in names}
        raw_full = [sem(f"raw_full{n}") for n in range(RAW)]
        table_built, table_out, out_done = map(sem, ("table_built", "table_out", "out_done"))
        bias_in = [sem(f"bias_in{n}") for n in range(2)]
        const_ready, ones_ready, pool_step = map(sem, ("const_ready", "ones_ready", "pool_step"))
        cact_ready, squared, rooted, diag_ready, lam_exp, lam_ready = map(
            sem, ("cact_ready", "squared", "rooted", "diag_ready", "lam_exp", "lam_ready"))
        v_step = sem("v_step")
        ada_step = sem("ada_step")
        sc1_ready, sh1_product, sh1_step, sh1_ready, mod_ready = map(
            sem, ("sc1_ready", "sh1_product", "sh1_step", "sh1_ready", "mod_ready"))
        var_ready, acc_ready, cols_ready, rows_ready, cols_read, rows_read = map(
            sem, ("var_ready", "acc_ready", "cols_ready", "rows_ready", "cols_read", "rows_read"))
        xT_ready, hT_even, hT_odd, h_high, h_split, proj_out = map(
            sem, ("xT_ready", "hT_even", "hT_odd", "h_high", "h_split", "proj_out"))
        group_high, group_low, group_done = map(sem, ("group_high", "group_low", "group_done"))
        scores_ready, logits_ready, max_ready, exp_done, attn_ready = map(
            sem, ("scores_ready", "logits_ready", "max_ready", "exp_done", "attn_ready"))
        pT_ready, pT_out, pv_done, pv_out, head_sq, nat_ready = map(
            sem, ("pT_ready", "pT_out", "pv_done", "pv_out", "head_sq", "nat_ready"))
        mixT_ready, mix_high, mix_split, x1_ready = map(sem, ("mixT_ready", "mix_high", "mix_split", "x1_ready"))
        x2T_ready, h2T_even, h2T_odd, h2_high, h2_split = map(
            sem, ("x2T_ready", "h2T_even", "h2T_odd", "h2_high", "h2_split"))
        q_out, s_ready, s_out = map(sem, ("q_out", "s_ready", "s_out"))
        gate_max, gate_exp, chosen_ready, cT_ready, cT_out = map(
            sem, ("gate_max", "gate_exp", "chosen_ready", "cT_ready", "cT_out"))
        high_ready, low_ready, block_used, act_ready, act_out = map(
            sem, ("high_ready", "low_ready", "block_used", "act_ready", "act_out"))
        oh2_ready, onehot_ready, gates_ready, gates_out = map(sem, ("oh2_ready", "onehot_ready", "gates_ready", "gates_out"))
        wh_ready, wl_ready, peer_ready, x2_ready, final_ready = map(
            sem, ("wh_ready", "wl_ready", "peer_ready", "x2_ready", "final_ready"))

        block = ctx.enter_context(nc.Block())

        GROUPS = [(n, col) for n in ("win0", "win1", "win2", "wo", "wq0", "wq1") for col in range(0, D, GW)]
        N_IN, N_OUT = 12, 4
        WO, WQ = N_IN, N_IN + N_OUT
        GIVES = [(kind, n * (GW if kind == "v" else 2)) for n in range(4) for kind in "qkv"]
        STEPS = [(g, e, third) for g in range(N_IN) for e in range(2) for third in range(3)]
        FIRST = 15
        FILL = [5, 4, 5, 4, 5, 4, 4, 4, 5, 4, 4, 5, 4]
        assert FIRST + sum(FILL) == len(STEPS) and len(FILL) == LATE

        def steps_at(a):
            return STEPS[FIRST + sum(FILL[:a]):FIRST + sum(FILL[:a + 1])]

        def done_at(a):
            return [g for g, e, third in steps_at(a) if (e, third) == (1, 2)]

        def early(g, a):
            return (g, 1, 2) in steps_at(a)[:3]

        def high_slot(w):
            return high_of[w % 2 if w < N_IN else 2 + w % 2]

        ADA = ["g1", "sc2", "sh2", "g2"]
        ada_w = {"g1": g1_w, "sc2": sc2_w, "sh2": sh2_w, "g2": g2_w}

        def unit(a):
            return a // 8, a // 2 % TT, a // 4 % 2 * 2 + a % 2

        def score_banks(a):
            return (3, 4) if a > LATE and (a - LATE) % 2 else (0, 1)

        def pT_bank(a):
            return 5 if a > LATE and (a - LATE) % 2 else 2

        def same_banks(a):
            return a if a <= LATE else a - 1

        def s_bank(g):
            return (4, 5, 2, 3)[g % 4]

        def place_pairs(c):
            return c // 2, c % 2 * SEQ

        def place_h(c):
            return c // 4 * 2 + c % 2, c % 4 // 2 * SEQ

        def place_h2(c):
            return (c + 4) % 8, 0

        @block.sync
        def _(sp):
            def load(name, dst, src):
                sp.dma_start(dst[:, :, :], src).then_inc(loaded[name], 16)

            sp.dma_start(ccol[:, :], c_col).then_inc(c_in, 16)
            sp.dma_start(small_cols[:, :], cols).then_inc(small_in, 16)
            sp.dma_start(lam_in[:, :], lam.broadcast_to([P, 4 * DH])).then_inc(lam_sem, 16)
            sp.dma_start(xs[:, :, :], x.rearrange("(t p) d -> p t d", p=P)).then_inc(x_in, 16)
            for e in range(PARTS):
                c = slice(e * GW, (e + 1) * GW)
                for n, (dst, src) in ((1, (sh1_w, w_ada[0])), (0, (sc1_w, w_ada[1]))):
                    sp.dma_start(dst[:, :, c], src[:, :, c]).then_inc(part_in[n][e], 16)

            def load_groups(name, src):
                for g in range(D // GW):
                    c = slice(g * GW, (g + 1) * GW)
                    sp.dma_start(full[name][:, :, c], src[:, :, c]).then_inc(win_in[name][g], 16)

            def load_bias(kind):
                m = kind * UNITS // 2
                sp.dma_start(bias[:, m:m + MAPS // 2, :],
                             bass.AP(tensor=scratch, offset=m * TABLE, ap=[[1, P], [TABLE, MAPS // 2], [1, SEQ]])
                             ).then_inc(bias_in[kind], 16)

            load_groups("win0", w_in[0])
            sp.wait_ge(table_out, 16)
            load_bias(0)
            sp.wait_ge(sc1_ready, PARTS)
            load_groups("win1", w_in[1])
            sp.wait_ge(sh1_ready, PARTS)
            load("win2", full["win2"], w_in[2])
            load_bias(1)
            sp.wait_ge(group_done, 4)
            load("g1", g1_w, w_ada[2])
            sp.wait_ge(group_done, 8)
            load("sc2", sc2_w, w_ada[4])
            sp.wait_ge(acc_ready, 1)
            load("wo", full["wo"], w_out)
            sp.wait_ge(group_done, N_IN)
            load("sh2", sh2_w, w_ada[3])
            sp.wait_ge(acc_ready, 2)
            load("wq0", full["wq0"], wq[0])
            sp.wait_ge(logits_ready, UNITS)
            load("keys", keys, keys_t)
            sp.wait_ge(nat_ready, TT)
            sp.dma_start(brow2[:, :], b_row[1:2, :]).then_inc(g2row_in, 16)
            sp.wait_ge(acc_ready, 3)
            load("wq1", full["wq1"], wq[1])
            sp.wait_ge(x1_ready, N_OUT)
            load("g2", g2_w, w_ada[5])
            sp.wait_ge(rows_ready, 3)
            sp.wait_ge(h2_split, DC // 2)
            for n in range(RAW):
                sp.dma_start(raw[:, n, :], u_t[n]).then_inc(raw_full[n], 16)
            with sp.Fori(1, BLOCKS // RAW) as turn:
                i = turn * RAW
                for s in range(RAW):
                    sp.wait_ge(low_ready, i + (s - RAW + 1))
                    sp.dma_start(raw[:, s, :], u_t[bass.ds(i + s, 1)].rearrange("a p d -> (a p) d")
                                 ).then_inc(raw_full[s], 16)
            with sp.Fori(0, BLOCKS // RAW) as turn:
                i = turn * RAW
                for s in range(RAW):
                    sp.wait_ge(low_ready, i + (BLOCKS + s - RAW + 1))
                    sp.dma_start(raw[:, s, :], v_b[bass.ds(i + s, 1)].rearrange("a p d -> (a p) d")
                                 ).then_inc(raw_full[s], 16)
            sp.wait_ge(wl_ready, BLOCKS)
            sp.wait_ge(wh_ready, BLOCKS)
            sp.dma_start(final_gb[:, :], final_g.broadcast_to([P, D])).then_inc(fin_in, 16)
            for t in range(TT):
                sp.wait_ge(final_ready, t + 1)
                sp.dma_start(out[t * P:(t + 1) * P, :], xs[:, t, :]).then_inc(out_done, 16)
            sp.wait_ge(out_done, 16 * TT)

        @block.gpsimd
        def _(pool):
            pool.dma_start(rel[:, :], rel_t).then_inc(rel_in, 16)
            nc.gpsimd.iota(iota[:, :], [[1, P]], base=0, channel_multiplier=0,
                           allow_small_or_imprecise_dtypes=True).then_inc(const_ready, 1)
            nc.gpsimd.memset(ident[:, :], 0.0).then_inc(pool_step, 1)
            pool.wait_ge(pool_step, 1)
            nc.gpsimd.affine_select(out=ident[:, :], in_=ident[:, :], compare_op=ALU.not_equal, fill=1.0,
                                    base=0, pattern=[[-1, P]], channel_multiplier=1).then_inc(const_ready, 1)
            nc.gpsimd.memset(table[:, 0:P - 1], MASKED).then_inc(table_built, 1)
            pool.wait_ge(rel_in, 16)
            half = REL_BUCKETS // 2
            nc.gpsimd.tensor_copy(table[:, P - 1:P - 1 + half], rel[:, 0:half]).then_inc(table_built, 1)
            for n, lo in enumerate(LOG_BUCKETS):
                hi = (LOG_BUCKETS + [SEQ])[n + 1]
                nc.gpsimd.tensor_copy(table[:, P - 1 + lo:P - 1 + hi],
                                      rel[:, half + n:half + n + 1].broadcast_to([MAPS, hi - lo])
                                      ).then_inc(table_built, 1)
            pool.wait_ge(table_built, 2 + len(LOG_BUCKETS))
            pool.dma_start(scratch.ap(), table[:, :]).then_inc(table_out, 16)
            for e in range(PARTS):
                w = sh1_w[:, :, e * GW:(e + 1) * GW]
                for n in range(2):
                    q = n * DC // 2
                    pool.wait_ge(sh1_product, e * DC + q + DC // 2)
                    nc.gpsimd.tensor_tensor(w[:, q:q + 2, :], w[:, q:q + 2, :], w[:, q + 2:q + 4, :], ALU.add
                                            ).then_inc(sh1_step, 1)
                pool.wait_ge(sh1_step, 3 * e + 2)
                nc.gpsimd.tensor_tensor(w[:, 0:2, :], w[:, 0:2, :], w[:, DC // 2:DC // 2 + 2, :], ALU.add
                                        ).then_inc(sh1_step, 1)
                pool.wait_ge(sh1_step, 3 * e + 3)
                nc.gpsimd.tensor_tensor(acc[:, 0, e * GW:(e + 1) * GW], w[:, 0, :], w[:, 1, :], ALU.add
                                        ).then_inc(sh1_ready, 1)
            for w, (name, col) in enumerate(GROUPS):
                if w == WO:
                    pool.wait_ge(pv_out, 1)
                    nc.gpsimd.tensor_tensor(head_junk[:, :, :].rearrange("p h d -> p (h d)"),
                                            diff_out[:, :, :].rearrange("p t d -> p (t d)"),
                                            diff_out[:, :, :].rearrange("p t d -> p (t d)"), ALU.mult
                                            ).then_inc(head_sq, 1)
                pool.wait_ge(group_high, w + 1)
                for e in range(2):
                    c = slice(col + e * P, col + (e + 1) * P)
                    nc.gpsimd.tensor_tensor(low_of[name][:, :, c], full[name][:, :, c],
                                            high_slot(w)[:, :, e * P:(e + 1) * P].bitcast(F32), ALU.subtract
                                            ).then_inc(group_low, 1)

            def low(n, s):
                pool.wait_ge(high_ready, n + 1)
                nc.gpsimd.tensor_tensor(split[:, s % 2, 1, :], raw[:, s, :],
                                        split[:, s % 2, 0, :].bitcast(F32), ALU.subtract).then_inc(low_ready, 1)

            with pool.Fori(0, (2 * BLOCKS) // TURN) as turn:
                i = turn * TURN
                for s in range(TURN):
                    low(i + s, s % RAW)

        @block.scalar
        def _(sc):
            sc.dma_start(brow1[:, :], b_row[0:1, :]).then_inc(g1row_in, 16)
            sc.wait_ge(c_in, 16)
            nc.scalar.activation(cact[:, :], ccol[:, :], ACT.Silu).then_inc(cact_ready, 1)

            sc.wait_ge(x_in, 16)
            for t in range(TT):
                nc.scalar.activation(nat[:, t, :], xs[:, t, :], ACT.Square, accum_out=sq[:, 0, t:t + 1]
                                     ).then_inc(squared, 1)
            sc.wait_ge(var_ready, 1)
            nc.scalar.activation(rstd[:, 0, :], sq[:, 0, :], ACT.Sqrt).then_inc(rooted, 1)
            sc.wait_ge(lam_ready, 2)
            nc.scalar.activation(lexp[:, :], lsum[:, :], ACT.Exp).then_inc(lam_exp, 1)

            def warm_table(n, func):
                sc.wait_ge(ones_ready, 1)
                nc.scalar.activation(warm[:, n:n + 1], ones[:, 0:1], func)

            def high_group(w):
                name, col = GROUPS[w]
                sc.wait_ge(win_in[name][w % 4] if name in win_in else loaded[name], 16)
                if w >= 2:
                    sc.wait_ge(group_done, w - 1)
                nc.scalar.activation(high_slot(w)[:, :, :], full[name][:, :, col:col + GW], ACT.Copy
                                     ).then_inc(group_high, 1)

            def high_columns(dst, a, b, nth, place, src_ready, even, odd, done):
                c = 2 * b
                sc.wait_ge(mod_ready, nth)
                n, col = place(c)
                sc.wait_ge(src_ready, c + 1 if place is place_h2 else c // 4 * 4 + 4)
                nc.scalar.activation(hT[:, c, :], bank[n][:, col:col + SEQ], ACT.Identity, scale=a[:, 0, c:c + 1],
                                     bias=a[:, 1, c:c + 1]).then_inc(even, 1)
                sc.wait_ge(even, b + 1)
                sc.wait_ge(odd, b + 1)
                nc.scalar.activation(dst[:, 0, c:c + 2, :], hT[:, c:c + 2, :], ACT.Copy).then_inc(done, 1)

            def shift_products(e):
                sc.wait_ge(part_in[1][e], 16)
                for c in range(DC):
                    w = sh1_w[:, c, e * GW:(e + 1) * GW]
                    nc.scalar.activation(w, w, ACT.Copy, scale=cact[:, c:c + 1]).then_inc(sh1_product, 1)

            def proj_copy(g):
                sc.wait_ge(group_done, g + 1)
                kind, n = GIVES[g]
                src = bank[4 - g % 2]
                if kind == "v":
                    if g == 2:
                        sc.wait_ge(lam_ready, 2)
                        sc.wait_ge(table_out, 16)
                    nc.scalar.activation(v[:, :, n:n + GW], src.rearrange("p (t n) -> p t n", t=TT), ACT.Copy
                                         ).then_inc(proj_out, 1)
                else:
                    n += PAIRS if kind == "k" else 0
                    nc.scalar.activation(qk[:, n:n + 2, :].rearrange("p a s -> p (a s)"), src, ACT.Copy,
                                         scale=QK_SCALE if kind == "q" else 1.0).then_inc(proj_out, 1)

            def exps(a):
                nk = (unit(a)[1] + 1) * P
                sc.wait_ge(max_ready, a + 1)
                if a >= 2:
                    sc.wait_ge(pT_ready, a - 1)
                for m in range(2):
                    nc.scalar.activation(prob[:, a % 2, m, 0:nk], logit[:, a % 2, m, 0:nk], ACT.Exp,
                                         bias=nmax[:, a, m:m + 1], accum_out=psum_[:, a, m:m + 1]
                                         ).then_inc(exp_done, 1)

            def pT_copy(a):
                moba, t, _ = unit(a)
                n = (t + 1) * (1 + moba)
                sc.wait_ge(pT_ready, a + 1)
                if a >= 2:
                    sc.wait_ge(pv_done, a - 1)
                nc.scalar.activation(probT[:, a % 2, 0:n, :].rearrange("p n q -> p (n q)"),
                                     bank[pT_bank(a)][:, 0:n * P], ACT.Copy).then_inc(pT_out, 1)

            sc.wait_ge(cact_ready, 1)
            shift_products(0)
            shift_products(1)
            for b in range(DC // 2):
                if b + 2 < PARTS:
                    shift_products(b + 2)
                if b == 2:
                    high_group(0)
                high_columns(hh, a1, b, b + 1, place_h, xT_ready, hT_even, hT_odd, h_high)
            sc.wait_ge(h_split, DC // 2)
            high_group(1)
            for g in range(FIRST // 6):
                proj_copy(g)
                high_group(g + 2)
            for a in range(UNITS):
                if a < LATE:
                    exps(a)
                    for g in (done_at(a - 1) if a else []):
                        if g + 2 < N_IN and not early(g, a - 1):
                            high_group(g + 2)
                    for g in done_at(a):
                        proj_copy(g)
                        if g + 2 < N_IN and early(g, a):
                            high_group(g + 2)
                elif a == LATE:
                    exps(a)
                if a >= LATE and a + 1 < UNITS:
                    exps(a + 1)
                pT_copy(a)
                if a == 8:
                    sc.wait_ge(pv_done, 8)
                    nc.scalar.activation(diff_out[:, :, :], banks[:, 6:8, :], ACT.Copy).then_inc(pv_out, 1)
                if a == UNITS - 2:
                    sc.wait_ge(var_ready, 2)
                    nc.scalar.activation(hrs[:, :], hsq[:, :], ACT.Sqrt).then_inc(rooted, 1)
            sc.wait_ge(scores_ready, UNITS)
            high_group(WO)
            high_group(WO + 1)
            for b in (2, 3):
                sc.wait_ge(mixT_ready, 2 * b + 2)
                nc.scalar.activation(hh[:, 0, 2 * b:2 * b + 2, :], bank[b].rearrange("p (c s) -> p c s", c=2),
                                     ACT.Copy).then_inc(mix_high, 1)
            high_group(WO + 2)
            high_group(WO + 3)
            for g in range(N_OUT):
                if g == 2:
                    high_group(WQ)
                sc.wait_ge(x1_ready, g + 1)
                cols = slice(g * GW, (g + 1) * GW)
                for t in range(TT):
                    nc.scalar.activation(nat[:, t, cols], xs[:, t, cols], ACT.Square,
                                         accum_out=sq_cols[:, t, g:g + 1]).then_inc(squared, 1)
            sc.wait_ge(var_ready, 3)
            nc.scalar.activation(rstd[:, 1, :], sq[:, 1, :], ACT.Sqrt).then_inc(rooted, 1)
            high_group(WQ + 1)
            for b in range(DC // 2):
                high_columns(h2r, a2, b, PARTS + 1 + b // 2, place_h2, x2T_ready, h2T_even, h2T_odd, h2_high)
            for g in range(LISTS // 2):
                sc.wait_ge(group_done, WQ + g + 1)
                nc.scalar.activation(qT[:, 2 * g:2 * g + 2, :].rearrange("p a s -> p (a s)"), bank[4 + g % 4],
                                     ACT.Copy).then_inc(q_out, 1)
                if WQ + g + 2 < len(GROUPS):
                    high_group(WQ + g + 2)
            warm_table(0, ACT.Gelu)
            def high(n, s, i):
                sc.wait_ge(raw_full[s], i * (16 // RAW) + 16)
                if not (isinstance(n, int) and n < 2):
                    sc.wait_ge(block_used, n - 1)
                nc.scalar.activation(split[:, s % 2, 0, :], raw[:, s, :], ACT.Copy).then_inc(high_ready, 1)

            for g in range(TT * LISTS // 4):
                t, l = g % 2, 4 * (g // 2)
                sc.wait_ge(s_ready, g + 1)
                nc.scalar.activation(score[:, t, l:l + 4, :].rearrange("p l n -> p (l n)"), bank[s_bank(g)],
                                     ACT.Copy).then_inc(s_out, 1)
                if g in (3, 5):
                    high((g - 3) // 2, (g - 3) // 2, 0)

            def gelu(n, s):
                sc.wait_ge(block_used, n + 1)
                nc.scalar.activation(act[:, bass.ds(n, 1), :].rearrange("p a s -> p (a s)"),
                                     bank[4 + s % 2][:, 0:SEQ], ACT.Gelu).then_inc(act_out, 1)

            def whigh(j, s):
                nc.scalar.activation(wsplit[:, s % 2, 0, :], act[:, bass.ds(j, 1), :].rearrange("p a s -> p (a s)"),
                                     ACT.Copy).then_inc(wh_ready, 1)

            def u_blocks(i):
                for s in range(RAW):
                    if not (isinstance(i, int) and i + s < 2):
                        high(i + s, s, i)
                    if not (isinstance(i, int) and i + s == 0):
                        gelu(i + (s - 1), s - 1)

            u_blocks(0)
            with sc.Fori(1, EXP_AT // RAW) as turn:
                i = turn * RAW
                u_blocks(i)
            for t in range(TT):
                sc.wait_ge(gate_max, t + 1)
                nc.scalar.activation(gate[:, t, :, :], gate[:, t, :, :], ACT.Exp).then_inc(gate_exp, 1)
            u_blocks(EXP_AT)
            with sc.Fori(EXP_AT // RAW + 1, HALF // RAW) as turn:
                i = turn * RAW
                u_blocks(i)
            sc.wait_ge(cT_out, TT)
            with sc.Fori(HALF // RAW, BLOCKS // RAW) as turn:
                i = turn * RAW
                u_blocks(i)
            for s in range(RAW):
                high(BLOCKS + s, s, BLOCKS)
                if s == 0:
                    gelu(BLOCKS - 1, RAW - 1)
                    sc.wait_ge(gates_out, NG)
                whigh(s, s)
            with sc.Fori(1, HALF // RAW) as turn:
                i = turn * RAW
                for s in range(RAW):
                    high(i + (BLOCKS + s), s, i + BLOCKS)
                    whigh(i + s, s)
            sc.wait_ge(gates_out, 2 * NG)
            with sc.Fori(HALF // RAW, BLOCKS // RAW) as turn:
                i = turn * RAW
                for s in range(RAW):
                    high(i + (BLOCKS + s), s, i + BLOCKS)
                    whigh(i + s, s)
            warm_table(1, ACT.Sqrt)
            for t in range(TT):
                sc.wait_ge(x2_ready, t + 1)
                nc.scalar.activation(end_junk[:, t, :], xs[:, t, :], ACT.Square,
                                     accum_out=sq[:, 2, t:t + 1]).then_inc(squared, 1)
                sc.wait_ge(var_ready, 4 + t)
                nc.scalar.activation(rstd[:, 2, t:t + 1], sq[:, 2, t:t + 1], ACT.Sqrt).then_inc(rooted, 1)

        @block.tensor
        def _(pe):
            def to_columns(src, done, chunks, place, scaled=False):
                for c in chunks:
                    for t in range(TT):
                        b, col = place(c)
                        dst, here = bank[b][:, col + t * P:col + (t + 1) * P], src[:, t, c * P:(c + 1) * P]
                        if scaled:
                            last = nc.tensor.matmul(dst, here, diag[:, t, :], start=True, stop=True)
                        else:
                            last = nc.tensor.transpose(dst, here, ident[:, :])
                    last.then_inc(done, 1)

            def first_columns(e):
                dst = bank[4 + e]
                for k, ready in enumerate((sc1_ready, sh1_ready)):
                    pe.wait_ge(ready, e + 1)
                    for n in range(2):
                        c = 2 * e + n
                        last = nc.tensor.matmul(dst[:, 2 * k + n:2 * k + n + 1], acc[:, 1 - k, c * P:(c + 1) * P],
                                                ones[:, 0:1], start=True, stop=True)
                last.then_inc(cols_ready, 1)

            def mod_column(k, col, two):
                pe.wait_ge(acc_ready, k + 1)
                for half in range(2):
                    for e in range(DC // 2):
                        c = half * DC // 2 + e
                        last = nc.tensor.matmul(bank[two[half]][:, col + e:col + e + 1],
                                                acc[:, k % 2, c * P:(c + 1) * P], ones[:, 0:1], start=True, stop=True)
                    last.then_inc(cols_ready, 1)

            def mod_row(src, brow, half, dst):
                cols = slice(half * 512, half * 512 + 512)
                nc.tensor.matmul(dst, ones[:, :], src[:, cols], start=True, stop=False)
                return nc.tensor.matmul(dst, ones[0:1, :], brow[0:1, cols], start=False, stop=True)

            def group_step(w, x, dst, rows, e, third, x_split=None):
                name, col = GROUPS[w]
                high, low = high_slot(w), low_of[name]
                out = dst[:, e * 256:(e + 1) * 256]
                here = slice(e * P, (e + 1) * P)
                if third < 2:
                    if e == 0 and third == 0:
                        pe.wait_ge(group_high, w + 1)
                    for c in range(third * DC // 2, (third + 1) * DC // 2):
                        if x_split is not None and e == 0 and c % 2 == 0:
                            pe.wait_ge(x_split, c // 2 + 1)
                        for part in range(2):
                            if rows:
                                nc.tensor.matmul(out, x[:, part, c, here], high[:, c, :],
                                                 start=(c == 0 and part == 0), stop=False)
                            else:
                                nc.tensor.matmul(out, high[:, c, here], x[:, part, c, :],
                                                 start=(c == 0 and part == 0), stop=False)
                    return
                pe.wait_ge(group_low, 2 * w + 2 if rows else 2 * w + 1 + e)
                for c in range(DC):
                    if rows:
                        last = nc.tensor.matmul(out, x[:, 0, c, here], low[:, c, col:col + GW],
                                                start=False, stop=(c == DC - 1))
                    else:
                        last = nc.tensor.matmul(out, low[:, c, col + e * P:col + (e + 1) * P], x[:, 0, c, :],
                                                start=False, stop=(c == DC - 1))
                if e == 1:
                    last.then_inc(group_done, 1)

            def group(w, x, dst, rows, x_split=None):
                for e in range(2):
                    for third in range(3):
                        group_step(w, x, dst, rows, e, third, x_split)

            def proj_step(g, e, third):
                if g >= 2 and (e, third) == (0, 0):
                    pe.wait_ge(proj_out, g - 1)
                group_step(g, hh, bank[4 - g % 2], GIVES[g][0] == "v", e, third, h_split if g == 0 else None)

            pe.wait_ge(diag_ready, TT)
            to_columns(xs, xT_ready, range(DC), place_h, scaled=True)
            for e in range(PARTS):
                first_columns(e)
            for step in STEPS[:FIRST]:
                proj_step(*step)

            def scores(a):
                moba, t, j = unit(a)
                j += DIFF_HEADS * moba
                nk = (t + 1) * P
                if a > 0:
                    pe.wait_ge(logits_ready, same_banks(a))
                for m in range(2):
                    rows = slice(m * DH, (m + 1) * DH)
                    last = nc.tensor.matmul(bank[score_banks(a)[m]][:, 0:nk], qk[rows, j, t * P:(t + 1) * P],
                                            qk[rows, PAIRS + j, 0:nk], start=True, stop=True)
                last.then_inc(scores_ready, 1)

            def transposes(a):
                moba, t, _ = unit(a)
                if moba:
                    pe.wait_ge(exp_done, 2 * (a + 1))
                else:
                    pe.wait_ge(attn_ready, a + 1)
                if a > 0:
                    pe.wait_ge(pT_out, same_banks(a))
                if a == LATE + 1:
                    pe.wait_ge(rows_read, 2)
                for m in range(1 + moba):
                    for kb in range(t + 1):
                        n = m * (t + 1) + kb
                        last = nc.tensor.transpose(bank[pT_bank(a)][:, n * P:(n + 1) * P],
                                                   prob[:, a % 2, m, kb * P:(kb + 1) * P], ident[:, :])
                last.then_inc(pT_ready, 1)

            def weigh(a):
                moba, t, j = unit(a)
                pe.wait_ge(pT_out, a + 1)
                if a % 4 == 0:
                    pe.wait_ge(proj_out, 3 * (a // 4 + 1))
                if a == 8:
                    pe.wait_ge(pv_out, 1)
                for m in range(1 + moba):
                    w, c0 = (DH, (2 * j + m) * DH) if moba else (P, j * P)
                    v0 = 512 * moba + c0
                    for kb in range(t + 1):
                        last = nc.tensor.matmul(bank[6 + t][:, c0:c0 + w], probT[:, a % 2, m * (t + 1) + kb, :],
                                                v[:, kb, v0:v0 + w], start=(kb == 0), stop=(kb == t))
                last.then_inc(pv_done, 1)

            pe.wait_ge(const_ready, 2)
            pe.wait_ge(proj_out, 2)
            scores(0)
            for a in range(UNITS):
                for step in steps_at(a) if a < LATE else []:
                    proj_step(*step)
                if a in (10, 11):
                    pe.wait_ge(acc_ready, 1)
                    pe.wait_ge(g1row_in, 16)
                    if a == 11:
                        pe.wait_ge(rows_read, 1)
                    mod_row(acc[:, 0, :], brow1, a - 10, bank[5]).then_inc(rows_ready, 1)
                transposes(a)
                if a < LATE:
                    if a % 4 == 3:
                        pe.wait_ge(proj_out, 3 * (a // 4 + 1) + 2)
                    scores(a + 1)
                if a == LATE - 1:
                    pe.wait_ge(proj_out, N_IN)
                if LATE - 1 <= a < UNITS - 2:
                    scores(a + 2)
                if a >= 1:
                    weigh(a - 1)
            weigh(UNITS - 1)

            pe.wait_ge(nat_ready, TT)
            to_columns(nat, mixT_ready, range(DC // 2), place_pairs)
            pe.wait_ge(nat_ready, 2 * TT)
            to_columns(nat, mixT_ready, range(DC // 2, DC), place_pairs)
            for g in range(N_OUT):
                group(WO + g, hh, bank[4 + g], True, mix_split if g == 0 else None)
            mod_column(1, 0, (0, 1))
            mod_column(2, DC // 2, (0, 1))
            pe.wait_ge(diag_ready, 2 * TT)
            pe.wait_ge(x1_ready, N_OUT)
            to_columns(xs, x2T_ready, range(DC // 2), place_h2, scaled=True)
            pe.wait_ge(cols_read, PARTS + 2)
            to_columns(xs, x2T_ready, range(DC // 2, DC), place_h2, scaled=True)

            for g in range(LISTS // 2):
                if g >= 4:
                    pe.wait_ge(q_out, g - 3)
                group(WQ + g, h2r, bank[4 + g % 4], False, h2_split if g == 0 else None)
                if g == 5:
                    pe.wait_ge(acc_ready, 4)
                    pe.wait_ge(g2row_in, 16)
                    for half in range(2):
                        last = mod_row(acc_g2, brow2, half, bank[half])
                    last.then_inc(rows_ready, 1)
            pe.wait_ge(loaded["keys"], 16)
            for g in range(TT * LISTS // 4):
                t, four = g % 2, g // 2
                if g in (0, 6):
                    pe.wait_ge(q_out, 6 if g == 0 else LISTS // 2)
                if g >= 4:
                    pe.wait_ge(s_out, g - 3)
                for e in range(4):
                    l = 4 * four + e
                    last = nc.tensor.matmul(bank[s_bank(g)][:, e * P:(e + 1) * P], qT[:, l, t * P:(t + 1) * P],
                                            keys[:, l, :], start=True, stop=True)
                last.then_inc(s_ready, 1)

            def u_block(n, s):
                pe.wait_ge(high_ready, n + 1)
                if not (isinstance(n, int) and n < 2):
                    pe.wait_ge(act_out, n - 1)
                dst = bank[4 + s % 2][:, 0:SEQ]
                for c in range(DC):
                    w = split[:, s % 2, 0, c * P:(c + 1) * P]
                    nc.tensor.matmul(dst, w, h2r[:, 0, c, :], start=(c == 0), stop=False)
                    nc.tensor.matmul(dst, w, h2r[:, 1, c, :], start=False, stop=False)
                pe.wait_ge(low_ready, n + 1)
                for c in range(DC):
                    last = nc.tensor.matmul(dst, split[:, s % 2, 1, c * P:(c + 1) * P], h2r[:, 0, c, :],
                                            start=False, stop=(c == DC - 1))
                last.then_inc(block_used, 1)

            def gates(n, s):
                pe.wait_ge(onehot_ready, n + 1)
                if not (isinstance(n, int) and n < 2):
                    pe.wait_ge(gates_out, n - 1)
                for k in range(GT):
                    for e in range(GP):
                        last = nc.tensor.matmul(bank[6 + s % 2][:, k * HALF:(k + 1) * HALF], oh1[:, s % 2, k, :],
                                                oh2g[:, s % 2, k, e, :], start=(e == 0), stop=(e == GP - 1))
                last.then_inc(gates_ready, 1)

            def v_high(s, t, first=False):
                for e in range(2):
                    for half in range(2):
                        nc.tensor.matmul(bank[2 * t + half][:, :], wsplit[:, s % 2, e, t * P:(t + 1) * P],
                                         split[:, s % 2, 0, half * 512:half * 512 + 512],
                                         start=first and e == 0, stop=False, skip_group_check=True)

            def v_low(s, t, last_block=False):
                for half in range(2):
                    last = nc.tensor.matmul(bank[2 * t + half][:, :], wsplit[:, s % 2, 0, t * P:(t + 1) * P],
                                            split[:, s % 2, 1, half * 512:half * 512 + 512],
                                            start=False, stop=last_block, skip_group_check=True)
                return last

            def v_ready(j):
                pe.wait_ge(high_ready, j + (BLOCKS + 1))
                pe.wait_ge(wh_ready, j + 1)
                pe.wait_ge(wl_ready, j + 1)

            def v_block(j, s, first=False):
                v_ready(j)
                for t in range(TT):
                    v_high(s, t, first)
                pe.wait_ge(low_ready, j + (BLOCKS + 1))
                for t in range(TT):
                    last = v_low(s, t)
                last.then_inc(block_used, 1)

            pe.wait_ge(s_out, 6)
            for s in range(TURN):
                u_block(s, s)
            with pe.Fori(1, TURN_AT // TURN) as turn:
                i = turn * TURN
                for s in range(TURN):
                    u_block(i + s, s)
            for t in range(TT):
                pe.wait_ge(chosen_ready, 1)
                for k in range(3):
                    last = nc.tensor.transpose(bank[6 + t][:, k * P:(k + 1) * P], chosen[:, t, k, :], ident[:, :])
                last.then_inc(cT_ready, 1)
            for s in range(HALF - TURN_AT):
                u_block(TURN_AT + s, s)
            pe.wait_ge(cT_out, TT)
            for s in range(TURN):
                if s % 2 == 0:
                    gates(s // 2, s // 2)
                u_block(HALF + s, s)
            with pe.Fori(1, HALF // TURN) as turn:
                i = turn * TURN
                g = turn * (TURN // 2)
                for s in range(TURN):
                    if s % 2 == 0:
                        gates(g + s // 2, s // 2)
                    u_block(i + (HALF + s), s)
            pe.wait_ge(rows_read, 3)
            pe.wait_ge(s_out, TT * LISTS // 4)
            for s in range(TURN):
                if s % 2 == 0:
                    gates(NG + s // 2, s // 2)
                v_block(s, s, first=(s == 0))
            with pe.Fori(1, HALF // TURN) as turn:
                i = turn * TURN
                g = turn * (TURN // 2)
                for s in range(TURN):
                    if s % 2 == 0:
                        gates(g + (NG + s // 2), s // 2)
                    v_block(i + s, s)
            with pe.Fori(HALF // TURN, (BLOCKS - TURN) // TURN) as turn:
                i = turn * TURN
                for s in range(TURN):
                    v_block(i + s, s)
            for s in range(TURN - 1):
                v_block(BLOCKS - TURN + s, s)
            v_ready(BLOCKS - 1)
            pe.wait_ge(low_ready, 2 * BLOCKS)
            for t in range(TT):
                v_high(RAW - 1, t)
                v_low(RAW - 1, t, last_block=True).then_inc(peer_ready, 1)

        @block.vector
        def _(ve):
            steps = [0]
            ada_steps = [0]

            def link(ins):
                steps[0] += 1
                ins.then_inc(v_step, 1)
                ve.wait_ge(v_step, steps[0])

            def add_chunk(dst, w, c, done=None):
                if c == 0:
                    ins = nc.vector.tensor_scalar(dst, w[:, 0, :], cact[:, 0:1], None, ALU.mult)
                else:
                    ve.wait_ge(ada_step, ada_steps[0])
                    ins = nc.vector.scalar_tensor_tensor(out=dst, in0=w[:, c, :], scalar=cact[:, c:c + 1],
                                                         in1=dst, op0=ALU.mult, op1=ALU.add)
                if c < DC - 1:
                    ins.then_inc(ada_step, 1)
                    ada_steps[0] += 1
                else:
                    ins.then_inc(done, 1)

            def ada(k, chunks):
                dst = acc_g2[:, :] if k == 3 else acc[:, k % 2, :]
                for c in chunks:
                    if c == 0:
                        ve.wait_ge(loaded[ADA[k]], 16)
                        if k < 2:
                            ve.wait_ge(cols_ready, PARTS)
                        if k == 2:
                            ve.wait_ge(rows_ready, 2)
                    add_chunk(dst, ada_w[ADA[k]], c, acc_ready)

            def root(n, nth, count):
                ve.wait_ge(squared, count)
                if n == 1:
                    link(nc.vector.tensor_reduce(sq[:, 1, :], sq_cols[:, :, :], AX.X, ALU.add))
                nc.vector.tensor_scalar(sq[:, n, :], sq[:, n, :], 1.0 / D, EPS, ALU.mult, ALU.add
                                        ).then_inc(var_ready, 1)
                ve.wait_ge(rooted, nth)
                link(nc.vector.reciprocal(rstd[:, n, :], rstd[:, n, :]))
                for t in range(TT):
                    nc.vector.tensor_scalar(diag[:, t, :], ident[:, :], rstd[:, n, t:t + 1], None, ALU.mult
                                            ).then_inc(diag_ready, 1)

            def modulate(a, n, c, cols, nth):
                ve.wait_ge(cols_ready, nth)
                ve.wait_ge(small_in, 16)
                read = PARTS * n + (c.stop - 1) * (PARTS if n == 0 else 2) // DC + 1
                nc.vector.tensor_tensor(a[:, :, c], cols.rearrange("p (a c) -> p a c", a=2),
                                        bcol[:, 2 * n:2 * n + 2, c], ALU.add).then_inc(cols_read, 1)
                ve.wait_ge(cols_read, read)
                nc.vector.scalar_tensor_tensor(out=a[:, 0, c], in0=a[:, 0, c], scalar=1.0, in1=gain[:, n, c],
                                               op0=ALU.add, op1=ALU.mult).then_inc(mod_ready, 1)

            def odd_chunk(a, b, nth, place, src_ready, odd):
                c = 2 * b + 1
                ve.wait_ge(mod_ready, nth)
                n, col = place(c)
                ve.wait_ge(src_ready, c + 1 if place is place_h2 else c // 4 * 4 + 4)
                nc.vector.tensor_scalar(hT[:, c, :], bank[n][:, col:col + SEQ], a[:, 0, c:c + 1], a[:, 1, c:c + 1],
                                        ALU.mult, ALU.add).then_inc(odd, 1)

            def rest(dst, b, high, done):
                two = slice(2 * b, 2 * b + 2)
                ve.wait_ge(high, b + 1)
                nc.vector.tensor_tensor(dst[:, 1, two, :], hT[:, two, :], dst[:, 0, two, :].bitcast(F32),
                                        ALU.subtract).then_inc(done, 1)

            nc.vector.memset(ones[:, :], 1.0).then_inc(ones_ready, 1)
            ve.wait_ge(lam_sem, 16)
            for n in range(2):
                nc.vector.tensor_tensor_reduce(out=lam_t[:, n, :], in0=lam_in[:, 2 * n * DH:(2 * n + 1) * DH],
                                               in1=lam_in[:, (2 * n + 1) * DH:(2 * n + 2) * DH], scale=1.0,
                                               scalar=0.0, op0=ALU.mult, op1=ALU.add,
                                               accum_out=lsum[:, n:n + 1]).then_inc(lam_ready, 1)
            ve.wait_ge(const_ready, 2)
            root(0, 1, TT)
            ve.wait_ge(cact_ready, 1)

            def first_scale(e):
                ve.wait_ge(part_in[0][e], 16)
                cols = slice(e * GW, (e + 1) * GW)
                for c in range(DC):
                    add_chunk(acc[:, 1, cols], sc1_w[:, :, cols], c, sc1_ready)

            def first_pair(b):
                modulate(a1, 0, slice(2 * b, 2 * b + 2), bank[4 + b][:, 0:4], b + 1)
                odd_chunk(a1, b, b + 1, place_h, xT_ready, hT_odd)

            first_scale(0)
            first_scale(1)
            for b in range(2):
                first_pair(b)
                first_scale(b + 2)
                rest(hh, b, h_high, h_split)
            first_pair(2)
            first_pair(3)
            rest(hh, 2, h_high, h_split)
            rest(hh, 3, h_high, h_split)
            ve.wait_ge(lam_exp, 1)
            link(nc.vector.scalar_tensor_tensor(out=neglam[:, :], in0=lexp[:, 1:2], scalar=-LAMBDA_INIT,
                                                in1=lexp[:, 0:1], op0=ALU.add, op1=ALU.subtract))
            nc.vector.tensor_scalar(sub08[:, :], sub, 1.0 - LAMBDA_INIT, None, ALU.mult)

            def logits(a):
                moba, t, j = unit(a)
                nk = (t + 1) * P
                m0 = 2 * (j + DIFF_HEADS * moba)
                b0 = score_banks(a)[0]
                ve.wait_ge(scores_ready, a + 1)
                if a >= 2:
                    ve.wait_ge(exp_done, 2 * (a - 1))
                if a == 8:
                    ve.wait_ge(bias_in[1], 16)
                nc.vector.tensor_tensor(logit[:, a % 2, :, 0:nk], banks[:, b0:b0 + 2, 0:nk],
                                        bias[:, m0:m0 + 2, 0:nk][:, :, ::-1], ALU.add).then_inc(logits_ready, 1)
                ve.wait_ge(logits_ready, a + 1)
                nc.vector.tensor_reduce(nmax[:, a, :], logit[:, a % 2, :, 0:nk], AX.X, ALU.max,
                                        negate=True).then_inc(max_ready, 1)

            def combine(a):
                _, t, j = unit(a)
                nk = (t + 1) * P
                ve.wait_ge(exp_done, 2 * (a + 1))
                link(nc.vector.reciprocal(rsum[:, a, :], psum_[:, a, :]))
                link(nc.vector.tensor_scalar(rlam[:, a:a + 1], rsum[:, a, 1:2], neglam[:, 0:1], None, ALU.mult))
                link(nc.vector.tensor_scalar(prob[:, a % 2, 1, 0:nk], prob[:, a % 2, 1, 0:nk], rlam[:, a:a + 1],
                                             None, ALU.mult))
                nc.vector.scalar_tensor_tensor(out=prob[:, a % 2, 0, 0:nk], in0=prob[:, a % 2, 0, 0:nk],
                                               scalar=rsum[:, a, 0:1], in1=prob[:, a % 2, 1, 0:nk],
                                               op0=ALU.mult, op1=ALU.add).then_inc(attn_ready, 1)

            def row_copy(n, src, dst):
                ve.wait_ge(rows_ready, n)
                nc.vector.tensor_copy(dst, src).then_inc(rows_read, 1)

            ve.wait_ge(bias_in[0], 16)
            SUMS = {6: (0, 0), 7: (0, 2), 8: (0, 4), 9: (0, 6), 10: (1, 0), 11: (1, 2), 12: (1, 4), 15: (1, 6)}

            def sums(a, n):
                if a in SUMS:
                    k, c = SUMS[a]
                    ada(k, range(c + n, c + n + 1))

            for a in range(8):
                logits(a)
                sums(a, 0)
                combine(a)
                sums(a, 1)
            logits(8)
            for a in range(8, UNITS):
                if a in (10, 11):
                    row_copy(a - 9, bank[5], g1b[:, (a - 10) * 512:(a - 9) * 512])
                if a < LATE:
                    sums(a, 0)
                    sums(a, 1)
                if a + 1 < UNITS:
                    logits(a + 1)
                if a == LATE:
                    ve.wait_ge(head_sq, 1)
                    link(nc.vector.tensor_reduce(hsq[:, :], head_junk[:, :, :], AX.X, ALU.add))
                    nc.vector.tensor_scalar(hsq[:, :], hsq[:, :], 1.0 / P, EPS, ALU.mult, ALU.add
                                            ).then_inc(var_ready, 1)
                if a == UNITS - 1:
                    sums(a, 0)
                    sums(a, 1)
                    ve.wait_ge(rooted, 2)
                    link(nc.vector.reciprocal(hrs[:, :], hrs[:, :]))
                    for t in range(TT):
                        nc.vector.tensor_tensor(nat[:, t, 0:512].rearrange("p (h d) -> p h d", d=P),
                                                diff_out[:, t, :].rearrange("p (h d) -> p h d", d=P),
                                                spread(hrs[:, t * DIFF_HEADS:(t + 1) * DIFF_HEADS], 2, P), ALU.mult
                                                ).then_inc(nat_ready, 1)

            ve.wait_ge(exp_done, 2 * UNITS)
            link(nc.vector.reciprocal(rsum[:, 8:UNITS, :], psum_[:, 8:UNITS, :]))
            for t in range(TT):
                ve.wait_ge(pv_done, 14 + 2 * t)
                inv = rsum[:, 8:UNITS, :].rearrange("p (n t j) m -> p t n (j m)", n=2, t=TT)[:, t]
                nc.vector.tensor_tensor(nat[:, t, 512:D].rearrange("p (n h d) -> p n h d", n=2, d=DH),
                                        bank[6 + t].rearrange("p (n h d) -> p n h d", n=2, d=DH),
                                        spread(inv, 3, DH), ALU.mult).then_inc(nat_ready, 1)
            for b in range(DC // 2):
                src = bank[b].rearrange("p (c s) -> p c s", c=2)
                two = slice(2 * b, 2 * b + 2)
                ve.wait_ge(mixT_ready, 2 * b + 2)
                if 2 * b < DIFF_HEADS:
                    link(nc.vector.tensor_scalar(hh[:, 0, two, :], src, sub08[:, 0:1], None, ALU.mult))
                    nc.vector.scalar_tensor_tensor(out=hh[:, 1, two, :], in0=src, scalar=sub08[:, 0:1],
                                                   in1=hh[:, 0, two, :].bitcast(F32), op0=ALU.mult,
                                                   op1=ALU.subtract).then_inc(mix_split, 1)
                else:
                    ve.wait_ge(mix_high, b - 1)
                    nc.vector.tensor_tensor(hh[:, 1, two, :], src, hh[:, 0, two, :].bitcast(F32),
                                            ALU.subtract).then_inc(mix_split, 1)
            ada(2, range(DC))
            for g in range(N_OUT):
                cols = slice(g * GW, (g + 1) * GW)
                ve.wait_ge(group_done, WO + g + 1)
                link(nc.vector.tensor_tensor(nat[:, :, cols], bank[4 + g].rearrange("p (t n) -> p t n", t=TT),
                                             spread(g1b[:, cols], 1, TT), ALU.mult))
                nc.vector.tensor_tensor(xs[:, :, cols], xs[:, :, cols], nat[:, :, cols], ALU.add
                                        ).then_inc(x1_ready, 1)
            root(1, 3, TT + TT * N_OUT)
            for half in range(2):
                modulate(a2, 1, slice(half * DC // 2, (half + 1) * DC // 2), bank[half][:, 0:DC], PARTS + 3 + half)
            for b in range(DC // 2):
                odd_chunk(a2, b, PARTS + 1 + b // 2, place_h2, x2T_ready, h2T_odd)
                if b:
                    rest(h2r, b - 1, h2_high, h2_split)
            rest(h2r, DC // 2 - 1, h2_high, h2_split)
            ada(3, range(DC))
            ve.wait_ge(rows_ready, 3)
            nc.vector.tensor_scalar(g2b[:, :], banks[:, 0:2, :].rearrange("p b n -> p (b n)"), 1.0 / GATE_SCALE,
                                    None, ALU.mult).then_inc(rows_read, 1)

            def top16(vals, idx, src, n):
                for k in range(0, TOPK, 8):
                    for l in range(n):
                        last = nc.vector.max(vals[:, l, k:k + 8], src(l))
                    link(last)
                    for l in range(n):
                        last = nc.vector.max_index(idx[:, l, k:k + 8], vals[:, l, k:k + 8], src(l))
                    link(last)
                    if k + 8 < TOPK:
                        for l in range(n):
                            last = nc.vector.match_replace(src(l), vals[:, l, k:k + 8], src(l), -3.0e38)
                        link(last)

            for t in range(TT):
                ve.wait_ge(s_out, TT * LISTS // 4 - 1 + t)
                if t == 0:
                    ve.wait_ge(s_ready, TT * LISTS // 4)
                top16(top_v, top_iu, lambda l: score[:, t, l, :], LISTS)
                link(nc.vector.tensor_copy(top_i[:, :, :], top_iu[:, :, :]))
                halves_v = top_v[:, :, :].rearrange("p (h two) k -> p two h k", two=2)
                halves_i = top_i[:, :, :].rearrange("p (h two) k -> p two h k", two=2)
                link(nc.vector.tensor_tensor(cand[:, :, :, :], spread(halves_v[:, 0], 3, TOPK),
                                             spread(halves_v[:, 1], 2, TOPK), ALU.add))
                top16(best, best_iu, lambda h: cand[:, h, :, :].rearrange("p a b -> p (a b)"), HEADS)
                nc.vector.tensor_tensor(gate[:, t, :, :], best[:, :, :],
                                        best[:, :, 0:1].broadcast_to([P, HEADS, TOPK]), ALU.subtract
                                        ).then_inc(gate_max, 1)
                nc.vector.tensor_scalar(part_u[:, 0, :, :], best_iu[:, :, :], 4, None, ALU.logical_shift_right)
                link(nc.vector.tensor_scalar(part_u[:, 1, :, :], best_iu[:, :, :], TOPK - 1, None,
                                             ALU.bitwise_and))
                link(nc.vector.tensor_copy(part[:, :, :, :], part_u[:, :, :, :]))
                for half in range(2):
                    place = spread(spread(iota[:, 0:TOPK], 1, TOPK), 1, HEADS)
                    link(nc.vector.tensor_tensor(hit[:, :, :, :], spread(part[:, half], 3, TOPK), place,
                                                 ALU.is_equal))
                    link(nc.vector.tensor_tensor(hit[:, :, :, :], hit[:, :, :, :],
                                                 spread(halves_i[:, half], 2, TOPK), ALU.mult))
                    link(nc.vector.tensor_reduce(chosen[:, t, half, :], hit[:, :, :, :], AX.X, ALU.add))
            ve.wait_ge(gate_exp, TT)
            link(nc.vector.tensor_reduce(gsum[:, :, :], gate[:, :, :, :], AX.X, ALU.add))
            link(nc.vector.tensor_scalar(gsum[:, :, :], gsum[:, :, :], 1.0 / GATE_SCALE, None, ALU.mult))
            link(nc.vector.reciprocal(gsum[:, :, :], gsum[:, :, :]))
            nc.vector.tensor_tensor(chosen[:, :, 2, :].rearrange("p t (h k) -> p t h k", k=TOPK),
                                    gate[:, :, :, :], spread(gsum[:, :, :], 3, TOPK), ALU.mult
                                    ).then_inc(chosen_ready, 1)
            for t in range(TT):
                ve.wait_ge(cT_ready, t + 1)
                nc.vector.tensor_copy(chosenT[:, :, t * P:(t + 1) * P],
                                      bank[6 + t][:, 0:3 * P].rearrange("p (k q) -> p k q", k=3)
                                      ).then_inc(cT_out, 1)
            ve.wait_ge(cT_out, TT)
            nc.vector.tensor_copy(iota_h[:, :], iota[:, :])
            link(nc.vector.tensor_copy(keys_h[:, :, :], chosenT[:, 0:2, :]))
            for e in range(GP):
                link(nc.vector.tensor_copy(part_h[:, :, e], chosenT[:, 2, :]))
                if e < GP - 1:
                    link(nc.vector.tensor_tensor(chosenT[:, 2, :], chosenT[:, 2, :], part_h[:, :, e],
                                                 ALU.subtract))

            def onehots(q, s, half):
                n = q + half * NG
                if not (isinstance(n, int) and n < 2):
                    ve.wait_ge(gates_ready, n - 1)
                toks = bass.ds(q * GT, GT)
                nc.vector.tensor_tensor(oh2[:, s % 2, :, :], spread(iota_h[:, half * HALF:(half + 1) * HALF], 1, GT),
                                        spread(keys_h[:, 1, toks], 2, HALF), ALU.is_equal).then_inc(oh2_ready, 1)
                nc.vector.tensor_tensor(oh1[:, s % 2, :, :], spread(iota_h[:, :], 1, GT),
                                        spread(keys_h[:, 0, toks], 2, KEYS), ALU.is_equal)
                ve.wait_ge(oh2_ready, n + 1)
                nc.vector.tensor_tensor(oh2g[:, s % 2, :, :, :], spread(oh2[:, s % 2, :, :], 2, GP),
                                        spread(part_h[:, toks, :], 3, HALF), ALU.mult).then_inc(onehot_ready, 1)

            def gate_acts(q, s, half):
                ve.wait_ge(gates_ready, q + (half * NG + 1))
                dst = act[:, half * HALF:(half + 1) * HALF, bass.ds(q * GT, GT)]
                nc.vector.tensor_tensor(dst, bank[6 + s % 2][:, 0:GT * HALF].rearrange("p (k j) -> p j k", k=GT),
                                        dst, ALU.mult).then_inc(gates_out, 1)

            def wlow(j, s):
                ve.wait_ge(wh_ready, j + 1)
                nc.vector.tensor_tensor(wsplit[:, s % 2, 1, :], act[:, bass.ds(j, 1), :].rearrange("p a s -> p (a s)"),
                                        wsplit[:, s % 2, 0, :].bitcast(F32), ALU.subtract).then_inc(wl_ready, 1)

            for s in range(RAW):
                onehots(s, s, 0)
                if s == 1:
                    ve.wait_ge(act_out, HALF)
                if s:
                    gate_acts(s - 1, s - 1, 0)
            with ve.Fori(1, NG // RAW) as turn:
                q = turn * RAW
                for s in range(RAW):
                    onehots(q + s, s, 0)
                    gate_acts(q + (s - 1), s - 1, 0)
            gate_acts(NG - 1, RAW - 1, 0)
            for s in range(RAW):
                onehots(s, s, 1)
                wlow(2 * s, 0)
                if s == 1:
                    ve.wait_ge(act_out, BLOCKS)
                if s:
                    gate_acts(s - 1, s - 1, 1)
                wlow(2 * s + 1, 1)
            with ve.Fori(1, NG // RAW) as turn:
                q = turn * RAW
                j = turn * (2 * RAW)
                for s in range(RAW):
                    onehots(q + s, s, 1)
                    wlow(j + 2 * s, 0)
                    gate_acts(q + (s - 1), s - 1, 1)
                    wlow(j + (2 * s + 1), 1)
            gate_acts(NG - 1, RAW - 1, 1)
            ve.wait_ge(gates_out, 2 * NG)
            with ve.Fori(HALF // RAW, BLOCKS // RAW) as turn:
                j = turn * RAW
                for s in range(RAW):
                    wlow(j + s, s)

            ve.wait_ge(wl_ready, BLOCKS)
            for t in range(TT):
                ve.wait_ge(peer_ready, t + 1)
                link(nc.vector.tensor_tensor(peer[:, t, :], banks[:, 2 * t:2 * t + 2, :].rearrange("p b n -> p (b n)"),
                                             g2b[:, :], ALU.mult))
                nc.vector.tensor_tensor(xs[:, t, :], xs[:, t, :], peer[:, t, :], ALU.add).then_inc(x2_ready, 1)
            ve.wait_ge(fin_in, 16)
            for t in range(TT):
                ve.wait_ge(squared, TT + TT * N_OUT + t + 1)
                nc.vector.tensor_scalar(sq[:, 2, t:t + 1], sq[:, 2, t:t + 1], 1.0 / D, EPS, ALU.mult, ALU.add
                                        ).then_inc(var_ready, 1)
                ve.wait_ge(rooted, 4 + t)
                link(nc.vector.reciprocal(rstd[:, 2, t:t + 1], rstd[:, 2, t:t + 1]))
                nc.vector.scalar_tensor_tensor(out=xs[:, t, :], in0=xs[:, t, :], scalar=rstd[:, 2, t:t + 1],
                                               in1=final_gb[:, :], op0=ALU.mult, op1=ALU.mult
                                               ).then_inc(final_ready, 1)


def kernel(x, c, rel_bias, w_ada, b_ada, norm1_g, w_in, diff_lambda, diff_subln_g,
           w_out, norm2_g, peer_wq, peer_keys, peer_u, peer_v, final_g):
    import numpy as np
    import concourse.bacc as bacc
    from concourse.bass_utils import run_bass_kernel_spmd

    def wide(w):
        w = np.asarray(w)
        return np.ascontiguousarray(w.reshape(DC, P, -1, D).transpose(2, 1, 0, 3))

    def column(w):
        w = np.asarray(w)
        return np.ascontiguousarray(np.moveaxis(w.reshape(w.shape[:-1] + (DC, P)), -1, 0))

    def heads_first(w):
        w = np.asarray(w)
        return w.reshape(D, 2, 3, 2, GW).transpose(0, 1, 3, 2, 4).reshape(D, 3 * D)

    maps = [m * DIFF_HEADS + j for j in range(DIFF_HEADS) for m in range(2)] + list(range(8, MAPS))
    b = np.asarray(b_ada)[0].reshape(6, D)
    rows = {
        "x": np.asarray(x)[0],
        "c_col": column(np.asarray(c)[0]),
        "rel_t": np.ascontiguousarray(np.asarray(rel_bias)[:, maps].T),
        "w_ada": wide(w_ada[0]),
        "b_row": np.ascontiguousarray(b[[2, 5]]),
        "cols": np.concatenate([column(b[[1, 0, 4, 3]]).reshape(P, -1), column(np.asarray(norm1_g)[0]),
                                column(np.asarray(norm2_g)[0]), np.asarray(diff_subln_g)[0].reshape(P, 1)], 1),
        "lam": np.ascontiguousarray(np.asarray(diff_lambda).reshape(1, 4 * DH)),
        "final_g": np.ascontiguousarray(np.asarray(final_g).reshape(1, D)),
        "w_in": wide(heads_first(w_in[0])),
        "w_out": wide(w_out[0])[0],
        "wq": wide(peer_wq[0]),
        "keys_t": np.ascontiguousarray(np.asarray(peer_keys)[0].reshape(LISTS, KEYS, P).transpose(2, 0, 1)),
        "u_t": np.ascontiguousarray(np.asarray(peer_u)[0].reshape(P, BLOCKS, DC, P).transpose(1, 3, 2, 0)
                                    ).reshape(BLOCKS, P, D),
        "v_b": np.ascontiguousarray(np.asarray(peer_v)[0].reshape(P, BLOCKS, D).transpose(1, 0, 2)),
    }
    nc = bacc.Bacc("TRN2", target_bir_lowering=False, num_devices=1)
    aps = {k: nc.dram_tensor(f"in_{k}", a.shape, F32, kind="ExternalInput").ap() for k, a in rows.items()}
    out = nc.dram_tensor("out", (SEQ, D), F32, kind="ExternalOutput").ap()
    hybrid_peer_layer(nc, out=out, **aps)
    r = run_bass_kernel_spmd(nc, [{f"in_{k}": a for k, a in rows.items()}], core_ids=[0])
    return r.results[0]["out"].reshape(1, SEQ, D)
```
